# Optimizing a Trainium2 kernel written in Bass

```python
import jax, jax.numpy as jnp
from jax import lax
import numpy as np

D_MODEL = 1024
BATCH = 1
SEQ = 128
DEPTH = 2
DEC_BATCH = 1
DEC_SEQ = 256
PAST_LEN = 128

GRID_W = 64
HEAD_DIM = 64
MIX_WIDTH = D_MODEL
GROUP_WIDTH = MIX_WIDTH // 4
ATTN_HEADS = GROUP_WIDTH // HEAD_DIM
ATTN_KV_HEADS = ATTN_HEADS // 2
ATTN_GROUP = ATTN_HEADS // ATTN_KV_HEADS
NA_HEADS = GROUP_WIDTH // HEAD_DIM
NA_KH = 8
NA_KW = 16
FOURIER_HEADS = 4
FOURIER_HEAD_W = GROUP_WIDTH // FOURIER_HEADS
POOL_WINDOWS = (2, 4, 8, 16)
POOL_GROUP_W = GROUP_WIDTH // len(POOL_WINDOWS)
Q_BLOCK = 128
ROPE_THETA = 10000.0
ATTN_SCALE = HEAD_DIM ** -0.5
PEER_HEADS = 8
PEER_N_KEYS = 128
PEER_N_EXPERTS = PEER_N_KEYS * PEER_N_KEYS
PEER_KEY_DIM = 256
PEER_TOPK = 16
PEER_CHUNK = 128
ALPHA = (2 * DEPTH) ** 0.25
BETA = (8 * DEPTH) ** -0.25
LN_EPS = 1e-6
RMS_EPS = 1e-6
ADA_CHUNKS = 6
A_Q_W = ATTN_HEADS * HEAD_DIM
A_KV_W = ATTN_KV_HEADS * HEAD_DIM
IN_SPLITS = (A_Q_W, A_KV_W, A_KV_W, GROUP_WIDTH, GROUP_WIDTH, GROUP_WIDTH, GROUP_WIDTH, GROUP_WIDTH)
P_IN = A_Q_W + 2 * A_KV_W + 5 * GROUP_WIDTH

kernel_name = "hybrid_diffusion_peer_step"

def layer_norm(x):
    xf = x.astype(jnp.float32)
    mu = xf.mean(-1, keepdims=True)
    var = jnp.square(xf - mu).mean(-1, keepdims=True)
    return (xf - mu) * lax.rsqrt(var + LN_EPS)

def modulate(x, shift, scale):
    return (layer_norm(x) * (1.0 + scale) + shift).astype(x.dtype)

def post_norm(z, g, b):
    return (layer_norm(z) * g + b).astype(z.dtype)

def head_rms_norm(x, g):
    xf = x.astype(jnp.float32)
    y = xf * lax.rsqrt(jnp.mean(jnp.square(xf), -1, keepdims=True) + RMS_EPS) * g
    return y.astype(x.dtype)

def axial_rope(x):
    L = x.shape[1]
    t = jnp.arange(L)
    row = (t // GRID_W).astype(jnp.float32)
    col = (t % GRID_W).astype(jnp.float32)
    nf = HEAD_DIM // 4
    inv = ROPE_THETA ** (-jnp.arange(nf, dtype=jnp.float32) / nf)

    def rot(xh, pos):
        ang = pos[:, None] * inv[None, :]
        cos = jnp.cos(ang)[:, None, :]
        sin = jnp.sin(ang)[:, None, :]
        x1, x2 = jnp.split(xh, 2, axis=-1)
        return jnp.concatenate([x1 * cos - x2 * sin, x1 * sin + x2 * cos], -1)

    xf = x.astype(jnp.float32)
    half = HEAD_DIM // 2
    return jnp.concatenate([rot(xf[..., :half], row), rot(xf[..., half:], col)], -1).astype(x.dtype)

def blocked_attention(q, k, v):
    B, Lq, Hkv, G, hd = q.shape
    nb = Lq // Q_BLOCK
    q_blocks = q.reshape(B, nb, Q_BLOCK, Hkv, G, hd).swapaxes(0, 1)

    def one_block(qb):
        s = jnp.einsum('bqhgd,bkhd->bhgqk', qb, k).astype(jnp.float32) * ATTN_SCALE
        p = jax.nn.softmax(s, axis=-1).astype(v.dtype)
        return jnp.einsum('bhgqk,bkhd->bqhgd', p, v)

    out = lax.map(one_block, q_blocks)
    return out.swapaxes(0, 1).reshape(B, Lq, Hkv * G * hd)

def neighbourhood_attention(q, k, v, k_ctx, v_ctx, bias_table):
    B, L, H, hd = q.shape
    rows = L // GRID_W
    kh = min(NA_KH, rows)
    n_win = kh * NA_KW
    row_ids = jnp.arange(rows)
    row_start = jnp.clip(row_ids - kh // 2, 0, rows - kh)
    col_ids = jnp.arange(GRID_W)
    col_keys = jnp.clip(col_ids - NA_KW // 2, 0, GRID_W - NA_KW)[:, None] + jnp.arange(NA_KW)[None, :]
    col_rel = col_keys - col_ids[:, None] + (NA_KW - 1)
    col_bias = bias_table[:, :, col_rel]
    kg = k.reshape(B, rows, GRID_W, H, hd)
    vg = v.reshape(B, rows, GRID_W, H, hd)
    q_rows = q.reshape(B, rows, GRID_W, H, hd).swapaxes(0, 1)

    def one_row(args):
        q_r, r, rs = args
        k_r = lax.dynamic_slice_in_dim(kg, rs, kh, axis=1)[:, :, col_keys]
        v_r = lax.dynamic_slice_in_dim(vg, rs, kh, axis=1)[:, :, col_keys]
        row_rel = rs + jnp.arange(kh) - r + (NA_KH - 1)
        bias = jnp.take(col_bias, row_rel, axis=1).transpose(0, 2, 1, 3)
        s_win = jnp.einsum('bqhd,bkqjhd->bhqkj', q_r, k_r).astype(jnp.float32) * ATTN_SCALE
        s_win = s_win + bias.astype(jnp.float32)[None]
        s_ctx = jnp.einsum('bqhd,bchd->bhqc', q_r, k_ctx).astype(jnp.float32) * ATTN_SCALE
        s = jnp.concatenate([s_win.reshape(B, H, GRID_W, n_win), s_ctx], axis=-1)
        p = jax.nn.softmax(s, axis=-1).astype(v.dtype)
        p_win = p[..., :n_win].reshape(B, H, GRID_W, kh, NA_KW)
        return (jnp.einsum('bhqkj,bkqjhd->bqhd', p_win, v_r)
                + jnp.einsum('bhqc,bchd->bqhd', p[..., n_win:], v_ctx))

    out = lax.map(one_row, (q_rows, row_ids, row_start))
    return out.swapaxes(0, 1).reshape(B, L, H * hd)

def fourier_mix(x, w):
    B, L, _ = x.shape
    xh = x.astype(jnp.float32).reshape(B, L, FOURIER_HEADS, FOURIER_HEAD_W)
    y = jnp.fft.fftn(xh, axes=(1, 3), norm="ortho").real
    return y.reshape(B, L, GROUP_WIDTH).astype(x.dtype) @ w

def multiscale_pool(x, w_pool, pool_scale):
    B, L, C = x.shape
    xf = x.astype(jnp.float32)
    cs = jnp.concatenate([jnp.zeros((B, 1, C), jnp.float32), jnp.cumsum(xf, axis=1)], axis=1)
    t = jnp.arange(L)
    outs = []
    for g, w in enumerate(POOL_WINDOWS):
        lo = jnp.clip(t - w // 2, 0, L)
        hi = jnp.clip(t - w // 2 + w, 0, L)
        sl = slice(g * POOL_GROUP_W, (g + 1) * POOL_GROUP_W)
        csg = cs[..., sl]
        mean = (csg[:, hi] - csg[:, lo]) / (hi - lo).astype(jnp.float32)[None, :, None]
        outs.append(mean - xf[..., sl])
    pooled = jnp.stack(outs, axis=2).astype(x.dtype)
    y = jnp.einsum('blgc,gcd->blgd', pooled, w_pool).reshape(B, L, C)
    return y * pool_scale

def peer(h, wq, k1, k2, u, v):
    B, L, D = h.shape
    T = B * L
    x = h.reshape(T, D)
    q = (x @ wq).reshape(T, PEER_HEADS, 2, PEER_KEY_DIM // 2)
    s1 = jnp.einsum('thd,nd->thn', q[:, :, 0], k1).astype(jnp.float32)
    s2 = jnp.einsum('thd,nd->thn', q[:, :, 1], k2).astype(jnp.float32)
    v1, i1 = lax.top_k(s1, PEER_TOPK)
    v2, i2 = lax.top_k(s2, PEER_TOPK)
    cand_s = (v1[..., :, None] + v2[..., None, :]).reshape(T, PEER_HEADS, PEER_TOPK * PEER_TOPK)
    cand_i = (i1[..., :, None] * PEER_N_KEYS + i2[..., None, :]).reshape(T, PEER_HEADS, PEER_TOPK * PEER_TOPK)
    top_s, pos = lax.top_k(cand_s, PEER_TOPK)
    idx = jnp.take_along_axis(cand_i, pos, axis=-1)
    g = jax.nn.softmax(top_s, axis=-1).astype(h.dtype)
    nck = T // PEER_CHUNK
    idx = idx.reshape(nck, PEER_CHUNK, PEER_HEADS * PEER_TOPK)
    g = g.reshape(nck, PEER_CHUNK, PEER_HEADS * PEER_TOPK)

    def one_chunk(args):
        xc, ic, gc = args
        a = jnp.einsum('td,tkd->tk', xc, u[ic])
        return jnp.einsum('tk,tkd->td', gc * jax.nn.gelu(a, approximate=False), v[ic])

    y = lax.map(one_chunk, (x.reshape(nck, PEER_CHUNK, D), idx, g))
    return y.reshape(B, L, D)

def trunk_layer(x, ada, lw, ctx_cache):
    B, L, _ = x.shape
    sh1, sc1, g1, sh2, sc2, g2 = jnp.split(ada, ADA_CHUNKS, axis=-1)
    h = modulate(x, sh1, sc1)
    proj = h @ lw["w_in"]
    parts = []
    off = 0
    for size in IN_SPLITS:
        parts.append(proj[..., off:off + size])
        off += size
    aq, ak, av, fx, nq, nk, nv, px = parts
    aq = head_rms_norm(aq.reshape(B, L, ATTN_HEADS, HEAD_DIM), lw["q_norm_g"])
    ak = head_rms_norm(ak.reshape(B, L, ATTN_KV_HEADS, HEAD_DIM), lw["k_norm_g"])
    av = av.reshape(B, L, ATTN_KV_HEADS, HEAD_DIM)
    nq = nq.reshape(B, L, NA_HEADS, HEAD_DIM)
    nk = nk.reshape(B, L, NA_HEADS, HEAD_DIM)
    nv = nv.reshape(B, L, NA_HEADS, HEAD_DIM)
    if ctx_cache is None:
        a_out = blocked_attention(aq.reshape(B, L, ATTN_KV_HEADS, ATTN_GROUP, HEAD_DIM), ak, av)
        n_out = blocked_attention(nq.reshape(B, L, NA_HEADS, 1, HEAD_DIM), nk, nv)
        ctx_kv = (ak, av, nk, nv)
    else:
        ck_a, cv_a, ck_n, cv_n = ctx_cache
        aq = axial_rope(aq)
        ak = axial_rope(ak)
        a_out = blocked_attention(aq.reshape(B, L, ATTN_KV_HEADS, ATTN_GROUP, HEAD_DIM),
                                  jnp.concatenate([ak, ck_a], axis=1),
                                  jnp.concatenate([av, cv_a], axis=1))
        n_out = neighbourhood_attention(nq, nk, nv, ck_n, cv_n, lw["na_bias"])
        ctx_kv = None
    f_out = fourier_mix(fx, lw["w_fourier"])
    p_out = multiscale_pool(px, lw["w_pool"], lw["pool_scale"])
    mix = jnp.concatenate([a_out, f_out, n_out, p_out], axis=-1) @ lw["w_out"]
    x = post_norm(ALPHA * x + g1 * mix, lw["ln1_g"], lw["ln1_b"])
    h2 = modulate(x, sh2, sc2)
    ff = peer(h2, lw["peer_wq"], lw["peer_k1"], lw["peer_k2"], lw["peer_u"], lw["peer_v"])
    x = post_norm(ALPHA * x + g2 * ff, lw["ln2_g"], lw["ln2_b"])
    return x, ctx_kv

def setup_inputs(seed: int = 0) -> dict:
    key = jax.random.key(seed)
    ks = jax.random.split(key, 32)
    D = D_MODEL

    def nrm(k, shape, s):
        return jax.random.normal(k, shape, jnp.float32) * s

    return {
        "x_prompt": nrm(ks[0], (BATCH, SEQ, D), 1.0),
        "x_sample": nrm(ks[1], (DEC_BATCH, DEC_SEQ, D), 1.0),
        "cache_attn_k": nrm(ks[2], (DEC_BATCH, DEPTH, PAST_LEN, ATTN_KV_HEADS, HEAD_DIM), 1.0),
        "cache_attn_v": nrm(ks[3], (DEC_BATCH, DEPTH, PAST_LEN, ATTN_KV_HEADS, HEAD_DIM), 1.0),
        "cache_na_k": nrm(ks[4], (DEC_BATCH, DEPTH, PAST_LEN, NA_HEADS, HEAD_DIM), 1.0),
        "cache_na_v": nrm(ks[5], (DEC_BATCH, DEPTH, PAST_LEN, NA_HEADS, HEAD_DIM), 1.0),
        "c": nrm(ks[6], (DEC_BATCH, D), 1.0),
        "c_ctx": nrm(ks[7], (D,), 1.0),
        "w_ada": nrm(ks[8], (DEPTH, D, ADA_CHUNKS * D), 0.5 * D ** -0.5),
        "b_ada": nrm(ks[9], (DEPTH, ADA_CHUNKS * D), 0.01),
        "w_in": nrm(ks[10], (DEPTH, D, P_IN), D ** -0.5),
        "q_norm_g": 1.0 + nrm(ks[11], (DEPTH, HEAD_DIM), 0.02),
        "k_norm_g": 1.0 + nrm(ks[12], (DEPTH, HEAD_DIM), 0.02),
        "w_fourier": nrm(ks[13], (DEPTH, GROUP_WIDTH, GROUP_WIDTH), GROUP_WIDTH ** -0.5),
        "na_bias": nrm(ks[14], (DEPTH, NA_HEADS, 2 * NA_KH - 1, 2 * NA_KW - 1), 0.1),
        "w_pool": nrm(ks[15], (DEPTH, len(POOL_WINDOWS), POOL_GROUP_W, POOL_GROUP_W), POOL_GROUP_W ** -0.5),
        "pool_scale": 1.0 + nrm(ks[16], (DEPTH, GROUP_WIDTH), 0.02),
        "w_out": nrm(ks[17], (DEPTH, MIX_WIDTH, D), MIX_WIDTH ** -0.5 * BETA),
        "ln1_g": 1.0 + nrm(ks[18], (DEPTH, D), 0.02),
        "ln1_b": nrm(ks[19], (DEPTH, D), 0.02),
        "ln2_g": 1.0 + nrm(ks[20], (DEPTH, D), 0.02),
        "ln2_b": nrm(ks[21], (DEPTH, D), 0.02),
        "peer_wq": nrm(ks[22], (DEPTH, D, PEER_HEADS * PEER_KEY_DIM), D ** -0.5),
        "peer_k1": nrm(ks[23], (DEPTH, PEER_N_KEYS, PEER_KEY_DIM // 2), (PEER_KEY_DIM // 2) ** -0.5),
        "peer_k2": nrm(ks[24], (DEPTH, PEER_N_KEYS, PEER_KEY_DIM // 2), (PEER_KEY_DIM // 2) ** -0.5),
        "peer_u": nrm(ks[25], (DEPTH, PEER_N_EXPERTS, D), D ** -0.5),
        "peer_v": nrm(ks[26], (DEPTH, PEER_N_EXPERTS, D), BETA),
    }

def reference(x_prompt, x_sample, cache_attn_k, cache_attn_v, cache_na_k, cache_na_v, c, c_ctx,
              w_ada, b_ada, w_in, q_norm_g, k_norm_g, w_fourier, na_bias, w_pool, pool_scale,
              w_out, ln1_g, ln1_b, ln2_g, ln2_b, peer_wq, peer_k1, peer_k2, peer_u, peer_v):
    xp = x_prompt
    xs = x_sample
    ak_list, av_list, nk_list, nv_list = [], [], [], []
    for l in range(DEPTH):
        lw = {
            "w_in": w_in[l], "q_norm_g": q_norm_g[l], "k_norm_g": k_norm_g[l],
            "w_fourier": w_fourier[l], "na_bias": na_bias[l], "w_pool": w_pool[l],
            "pool_scale": pool_scale[l], "w_out": w_out[l],
            "ln1_g": ln1_g[l], "ln1_b": ln1_b[l], "ln2_g": ln2_g[l], "ln2_b": ln2_b[l],
            "peer_wq": peer_wq[l], "peer_k1": peer_k1[l], "peer_k2": peer_k2[l],
            "peer_u": peer_u[l], "peer_v": peer_v[l],
        }
        ada_ctx = (jax.nn.silu(c_ctx[None, :]) @ w_ada[l] + b_ada[l])[:, None, :]
        ada_lat = (jax.nn.silu(c) @ w_ada[l] + b_ada[l])[:, None, :]
        xp, (ak, av, nk, nv) = trunk_layer(xp, ada_ctx, lw, None)
        ak_list.append(ak)
        av_list.append(av)
        nk_list.append(nk)
        nv_list.append(nv)
        xs, _ = trunk_layer(xs, ada_lat, lw,
                            (cache_attn_k[:, l], cache_attn_v[:, l], cache_na_k[:, l], cache_na_v[:, l]))
    new_attn_k = jnp.stack(ak_list, axis=1)
    new_attn_v = jnp.stack(av_list, axis=1)
    new_na_k = jnp.stack(nk_list, axis=1)
    new_na_v = jnp.stack(nv_list, axis=1)
    return (xp, xs, new_attn_k, new_attn_v, new_na_k, new_na_v)


_drawn_inputs = setup_inputs


def setup_inputs(seed=0):
    import zlib

    import numpy as np

    out = dict(_drawn_inputs(seed))
    spreads = {}
    factors = {'cache_attn_k': 8.0,
     'cache_attn_v': 8.0,
     'cache_na_k': 6.636,
     'cache_na_v': 5.597,
     'b_ada': 3.847,
     'q_norm_g': 8.0,
     'k_norm_g': 9.226,
     'na_bias': 64.0,
     'pool_scale': 22.957}
    for name, (base, spread) in spreads.items():
        noise = np.random.default_rng([zlib.crc32(name.encode()), seed]).standard_normal(out[name].shape)
        drawn = base * np.exp(spread * noise) if base else spread * noise
        out[name] = __import__('jax').numpy.asarray(drawn.astype(out[name].dtype))
    for name, factor in factors.items():
        out[name] = (out[name] * factor).astype(out[name].dtype)
    return out
```

```python
from contextlib import ExitStack

import concourse.bass as bass
from concourse import mybir

F32 = mybir.dt.float32
U32 = mybir.dt.uint32
ALU = mybir.AluOpType
ACT = mybir.ActivationFunctionType
AX_X = mybir.AxisListType.X

P = 128
D = 1024
KC = D // P
DEPTH = 2
HD = 64
GRID_W = 64
NA_KH = 8
NA_KW = 16
NB = 3
T = NB * P
KEYS = T + P
HEADS = 8
TOPK = 16
PICKS = HEADS * TOPK
N_KEYS = 128
EXPERTS = N_KEYS * N_KEYS
ALPHA = (2 * DEPTH) ** 0.25
EPS = 1e-6
WT = 256
RING = 4
SLOTS = 4
GROUP = 4
BODY = 4
LOW = -3.0e38
ADA_T, IN_T, OUT_T, Q_T = 24, 7, 4, 8
LAYER_T = ADA_T + IN_T + OUT_T + Q_T
SH1, SC1, G1, SH2, SC2, G2 = (KC * i for i in range(6))
T_AQ, T_AKV, T_FX, T_NQ, T_NK, T_NV, T_PX = range(7)
JOBS = [(b, m, h) for b in range(NB) for m in range(2) for h in range(4)]
KEY_LO = [0, P, P]
KEY_HI = [P, KEYS, KEYS]


TURNS = 2 + NB + 1 + NB + 2 + 2 * NB
INS = 5 * NB + 4


def turn_at(l, what, b):
    return 1 + TURNS * l + {"ln1": 3 + b, "qk": 7 + b, "ln2": 12 + 2 * b, "back": 13 + 2 * b}[what]


def in_at(l, j, b):
    before = sum(2 if i in (T_NQ, T_NK) else NB for i in range(j))
    return INS * l + before + b + 1


def stream(b):
    return 0 if b == 0 else 1


class Steps:

    def __init__(self, eng):
        self.eng, self.taken, self.given = eng, {}, {}

    def take(self, sem, n=1, unit=1):
        k = self.taken[sem.name] = self.taken.get(sem.name, 0) + n
        self.eng.wait_ge(sem, k * unit)

    def free(self, sem, depth):
        k = self.taken[sem.name] = self.taken.get(sem.name, 0) + 1
        if k > depth:
            self.eng.wait_ge(sem, k - depth)

    def give(self, ins, sem):
        self.given[sem.name] = self.given.get(sem.name, 0) + 1
        ins.then_inc(sem, 1)

    def step(self, ins, sem):
        self.give(ins, sem)
        self.eng.wait_ge(sem, self.given[sem.name])


def program(nc, ins, outs):
    with ExitStack() as ctx:
        def sb(name, shape, dt=F32):
            return ctx.enter_context(nc.sbuf_tensor(name, shape, dt))

        def sem(name):
            return ctx.enter_context(nc.semaphore(name))

        ps = ctx.enter_context(nc.psum_tensor("ps", [P, 8, 512], F32))
        ps_turn = ps[:, 0:2, :].rearrange("p a n -> p (a n)")
        ps_proj = [ps[:, 2 + i, :] for i in range(2)]
        ps_sc = [ps[:, 4 + i, :] for i in range(2)]
        ps_pt = ps[:, 6, :]
        ps_o = ps[:, 7, :]
        ps_top = ps[:, 4:6, :].rearrange("p a n -> p (a n)")
        ps_y = ps_turn

        x = sb("x", [P, NB, D])
        hT = sb("hT", [P, KC, T])
        xhat = sb("xhat", [P, D])
        h2 = sb("h2", [P, NB, D])
        mixT = sb("mixT", [P, KC, T])
        ring = sb("ring", [P, RING, KC, WT])
        ada_raw = sb("ada_raw", [P, 146])
        p_scale = ada_raw[:, 144:146]
        ada = sb("ada", [P, 6 * KC, 2])
        gate = sb("gate", [P, 2, D])
        ln_g = sb("ln_g", [P, D])
        ln_b = sb("ln_b", [P, D])
        stats = sb("stats", [P, 2, 6])
        mv = sb("mv", [P, 2])
        std = sb("std", [P, 1])
        rstd = sb("rstd", [P, 1])
        ident = sb("ident", [P, P])
        eps = sb("eps", [P, 1])
        zeros = sb("zeros", [P, P])
        crow = sb("crow", [2 * KC, P])
        silu_c = sb("silu_c", [P, 2, KC])
        dftL = sb("dftL", [P, 2, 2, 2 * P])
        dftP = sb("dftP", [P, 2, P])
        dftC = sb("dftC", [P, 2, P])
        poolL = sb("poolL", [P, 4, 2, 2 * P])
        poolP = sb("poolP", [P, 4, P])
        rope = sb("rope", [P, 2, 2, HD])
        na_mask = sb("na_mask", [P, 2, 2 * P])
        iota16 = sb("iota16", [P, TOPK])
        b_row = sb("b_row", [6 * KC + 2, P])
        qk_g = sb("qk_g", [P, 6, HD])
        na_b = sb("na_b", [P, 2, 4, 3 * P])
        wf = sb("wf", [P, 2, 2 * P])
        wp = sb("wp", [P, 2, HD])
        cache_k = sb("cache_k", [P, 3 * P])
        k12 = sb("k12", [P, 2, P])
        k12T = sb("k12T", [P, 2, P])
        qk = sb("qk", [P, NB, 6, HD])
        av = sb("av", [P, 4, P])
        nv = sb("nv", [P, 4, 2 * P])
        nk_out = sb("nk_out", [P, 2 * P])
        aqT = sb("aqT", [P, 2, T])
        akT = sb("akT", [P, KEYS])
        nqT = sb("nqT", [P, 2, T])
        nkT = sb("nkT", [P, 2, KEYS])
        ss = sb("ss", [P, 6])
        ss2 = sb("ss2", [P, 6])
        room = sb("room", [P, 2 * SLOTS * D])
        at = [0]

        def part(shape):
            n = 1
            for s in shape:
                n *= s
            v = room[:, at[0]:at[0] + n]
            at[0] += n
            assert at[0] <= 2 * SLOTS * D
            return v

        fx = part([NB, 2 * P]).rearrange("p (b n) -> p b n", b=NB)
        px = part([NB, 2 * P]).rearrange("p (b n) -> p b n", b=NB)
        dT = part([2, 2, T]).rearrange("p (c m n) -> p c m n", c=2, m=2)
        yT = part([2, T]).rearrange("p (c n) -> p c n", c=2)
        poolT = part([2, T]).rearrange("p (c n) -> p c n", c=2)
        score = part([2, 3 * P]).rearrange("p (s n) -> p s n", s=2)
        prob = part([2, 3 * P]).rearrange("p (s n) -> p s n", s=2)
        probT = part([2, 3 * P]).rearrange("p (s n) -> p s n", s=2)
        qkn, sq, rot = (part([6, HD]).rearrange("p (h d) -> p h d", h=6) for _ in range(3))
        at[0] = 0
        u_rows = part([SLOTS, D]).rearrange("p (s n) -> p s n", s=SLOTS)
        v_rows = part([SLOTS, D]).rearrange("p (s n) -> p s n", s=SLOTS)

        nmax = sb("nmax", [P, 2])
        psums = sb("psums", [P, 2])
        pinv = sb("pinv", [P, 2])
        qT = nqT
        best = sb("best", [P, NB, 2, HEADS, TOPK])
        best_i = sb("best_i", [P, NB, 2, HEADS, TOPK], U32)
        n_cand = HEADS * TOPK * TOPK
        mix_flat, h_flat = (t[:].rearrange("p k n -> p (k n)") for t in (mixT, hT))
        cand = mix_flat[:, 0:n_cand].rearrange("p (h n) -> p h n", h=HEADS)
        scr = mix_flat[:, n_cand:n_cand + NB * 2 * N_KEYS].rearrange("p (i n) -> p i n", i=NB * 2)
        cand2 = h_flat[:, 0:n_cand].rearrange("p (h n) -> p h n", h=HEADS)
        top = sb("top", [P, HEADS, TOPK])
        pos = h_flat[:, n_cand:n_cand + PICKS].bitcast(U32).rearrange("p (h k) -> p h k", h=HEADS)
        pos_ij, pos_f, best_f = (h_flat[:, n_cand + i * PICKS:n_cand + (i + 2) * PICKS] for i in (1, 3, 5))
        pos_ij, pos_f, best_f, found = (t.rearrange("p (a h k) -> p a h k", a=2, h=HEADS) for t in (
            pos_ij.bitcast(U32), pos_f, best_f, mix_flat[:, n_cand + 768:n_cand + 1024]))
        idx_f = sb("idx_f", [P, PICKS])
        idx = sb("idx", [P, PICKS], U32)
        cur = sb("cur", [P, BODY, GROUP], U32)
        gsum = sb("gsum", [P, HEADS])
        gw = sb("gw", [P, HEADS, TOPK])
        dots = sb("dots", [P, GROUP])
        gelu = sb("gelu", [P, GROUP])
        weight = sb("weight", [P, GROUP])
        junk = xhat
        diag = sb("diag", [P, SLOTS, P])

        w_landed = [sem(f"w_landed{i}") for i in range(RING)]
        w_used = sem("w_used")
        consts_in = sem("consts_in")
        small_in = sem("small_in")
        small_used = sem("small_used")
        ln1_in = sem("ln1_in")
        ln2_in = sem("ln2_in")
        ln1_used = sem("ln1_used")
        ln2_used = sem("ln2_used")
        pool_ready = sem("pool_ready")
        turn_ready = sem("turn_ready")
        turn_free = sem("turn_free")
        proj_ready = sem("proj_ready")
        proj_free = sem("proj_free")
        ada_raw_ready = sem("ada_raw_ready")
        ada_ready = sem("ada_ready")
        gate_ready = sem("gate_ready")
        gate_used = sem("gate_used")
        dve_step = sem("dve_step")
        var_ready = sem("var_ready")
        std_ready = sem("std_ready")
        xhat_ready = sem("xhat_ready")
        hT_ready = sem("hT_ready")
        h2_ready = sem("h2_ready")
        in_ready = sem("in_ready")
        ss_ready = sem("ss_ready")
        srt_ready = sem("srt_ready")
        qkn_ready = sem("qkn_ready")
        k_out_ready = sem("k_out_ready")
        k_out_done = sem("k_out_done")
        att_in_ready = sem("att_in_ready")
        nk_out_ready = sem("nk_out_ready")
        bias_ready = sem("bias_ready")
        side_ready = sem("side_ready")
        mix_side_ready = sem("mix_side_ready")
        s_ready = sem("s_ready")
        s_free = sem("s_free")
        score_ready = sem("score_ready")
        nmax_ready = sem("nmax_ready")
        exp_ready = sem("exp_ready")
        prob_ready = sem("prob_ready")
        pt_ready = sem("pt_ready")
        probT_ready = sem("probT_ready")
        o_ready = sem("o_ready")
        o_free = sem("o_free")
        mo_ready = sem("mo_ready")
        mo_free = sem("mo_free")
        qT_ready = sem("qT_ready")
        top_ready = sem("top_ready")
        top_free = sem("top_free")
        gexp_in = sem("gexp_in")
        gexp_out = sem("gexp_out")
        idx_ready = sem("idx_ready")
        cur_ready = sem("cur_ready")
        pool_pace = sem("pool_pace")
        u_landed = [sem(f"u_landed{i}") for i in range(SLOTS)]
        v_landed = [sem(f"v_landed{i}") for i in range(SLOTS)]
        u_free = sem("u_free")
        v_free = sem("v_free")
        gelu_ready = sem("gelu_ready")
        weight_ready = sem("weight_ready")
        diag_ready = sem("diag_ready")
        y_cleared = sem("y_cleared")
        y_free = sem("y_free")
        x_ready = sem("x_ready")
        out_done = sem("out_done")

        w_view = [w.rearrange("l (k p) n -> l p k n", p=P)
                  for w in (ins["w_ada"], ins["w_in"], ins["w_out"], ins["peer_wq"])]
        table_u = ins["peer_u"].rearrange("l e d -> (l e) d")
        table_v = ins["peer_v"].rearrange("l e d -> (l e) d")

        block = ctx.enter_context(nc.Block())

        @block.sync
        def _(sp):
            st = Steps(sp)
            n = 0
            for l in range(DEPTH):
                for w, tiles in zip(w_view, (ADA_T, IN_T, OUT_T, Q_T)):
                    for j in range(tiles):
                        st.free(w_used, RING)
                        sp.dma_start(ring[:, n % RING], w[l][:, :, j * WT:(j + 1) * WT]).then_inc(w_landed[n % RING], 16)
                        n += 1

        @block.gpsimd
        def _(pool):
            st = Steps(pool)
            nc.gpsimd.memset(zeros[:], 0.0)
            nc.gpsimd.memset(eps[:], EPS)
            st.give(nc.gpsimd.iota(iota16[:], [[1, TOPK]], base=0, channel_multiplier=0,
                                   allow_small_or_imprecise_dtypes=True), pool_ready)
            pool.sem_inc(u_free, SLOTS)
            pool.sem_inc(v_free, SLOTS)
            for l in range(DEPTH):
                st.take(small_in, 1, 16 * 35)
                for qb in range(2):
                    for h in range(4):
                        ins_ = nc.gpsimd.tensor_tensor(na_b[:, qb, h, 0:2 * P], na_b[:, qb, h, 0:2 * P],
                                                       na_mask[:, qb, :], ALU.add)
                ins_ = nc.gpsimd.memset(na_b[:, :, :, 2 * P:3 * P], 0.0)
                st.give(ins_, bias_ready)
                for b in range(NB):
                    step = l * NB + b
                    st.take(idx_ready)
                    rows0 = step * PICKS // SLOTS

                    def copy_cur(base, g):
                        ins_ = nc.gpsimd.tensor_copy(cur[:, g % BODY, :], idx[:, bass.ds(base * BODY * GROUP + g * GROUP, GROUP)]
                                                     if not isinstance(base, int) else
                                                     idx[:, (base * BODY + g) * GROUP:(base * BODY + g + 1) * GROUP])
                        ins_.then_inc(cur_ready, 1)
                        pool.wait_ge(cur_ready, step * (PICKS // GROUP) + base * BODY + g + 1)
                        pool.sem_inc(pool_pace, 1)

                    def gather_u(base, g, m):
                        pool.wait_ge(u_free, step * PICKS + base * (BODY * GROUP) + g * GROUP + m + 1)
                        pool.sem_inc(pool_pace, 1)
                        nc.gpsimd.indirect_dma_start(u_rows[:, m, :], None, table_u,
                                                     bass.IndirectOffsetOnAxis(cur[:, g % BODY, m:m + 1], 0)).then_inc(u_landed[m], 16)

                    def gather_v(base, g, m):
                        pool.wait_ge(v_free, step * PICKS + base * (BODY * GROUP) + g * GROUP + m + 1)
                        pool.sem_inc(pool_pace, 1)
                        nc.gpsimd.indirect_dma_start(v_rows[:, m, :], None, table_v,
                                                     bass.IndirectOffsetOnAxis(cur[:, g % BODY, m:m + 1], 0)).then_inc(v_landed[m], 16)

                    def body(base, last):
                        for g in range(BODY):
                            ahead = not (last and g == BODY - 1)
                            if ahead:
                                copy_cur(base, g + 1)
                            for m in range(GROUP):
                                if ahead:
                                    gather_u(base, g + 1, m)
                                gather_v(base, g, m)

                    copy_cur(0, 0)
                    for m in range(GROUP):
                        gather_u(0, 0, m)
                    with pool.Fori(0, PICKS // (BODY * GROUP) - 1) as i:
                        body(i, False)
                    body(PICKS // (BODY * GROUP) - 1, True)

        @block.scalar
        def _(act):
            st = Steps(act)

            def load(dst, src, s):
                act.dma_start(dst, src).then_inc(s, 16)

            def load_small(l):
                load(b_row[0:6 * KC, :], ins["b_ada"][l].rearrange("(k p) -> k p", p=P), small_in)
                load(cache_k[:, 0:P], ins["cache_attn_k"][0, l].rearrange("t h d -> t (h d)"), small_in)
                load(cache_k[:, P:3 * P], ins["cache_na_k"][0, l].rearrange("t h d -> t (h d)"), small_in)
                load(av[:, 3, :], ins["cache_attn_v"][0, l].rearrange("t h d -> t (h d)"), small_in)
                load(nv[:, 3, :], ins["cache_na_v"][0, l].rearrange("t h d -> t (h d)"), small_in)
                for h in range(6):
                    g = ins["q_norm_g" if h < 4 else "k_norm_g"][l:l + 1, :]
                    load(qk_g[:, h, :], g.to_broadcast([P, HD]), small_in)
                load(wf[:], ins["w_fourier"][l].rearrange("(c p) n -> p c n", p=P), small_in)
                for g in range(4):
                    load(wp[64 * (g % 2):64 * (g % 2) + 64, g // 2, :], ins["w_pool"][l, g], small_in)
                load(b_row[6 * KC:6 * KC + 2, :], ins["pool_scale"][l].rearrange("(c p) -> c p", p=P), small_in)
                load(k12[:, 0, :], ins["peer_k1"][l], small_in)
                load(k12[:, 1, :], ins["peer_k2"][l], small_in)
                for r in range(4):
                    for h in range(4):
                        load(na_b[64 * (r % 2):64 * (r % 2) + 64, r // 2, h, 0:2 * P].rearrange("p (a b) -> p a b", a=4),
                             ins["na_bias_slid"][l, h, :, NA_KH - 1 - r:NA_KH + 3 - r, :], small_in)

            def load_ln(l, which, s):
                load(ln_g[:], ins[f"ln{which}_g"][l:l + 1, :].to_broadcast([P, D]), s)
                load(ln_b[:], ins[f"ln{which}_b"][l:l + 1, :].to_broadcast([P, D]), s)

            load(ident[:], ins["const_ident"], consts_in)
            load(crow[0:KC, :], ins["c_ctx"].rearrange("(k p) -> k p", p=P), consts_in)
            load(crow[KC:2 * KC, :], ins["c"][0].rearrange("(k p) -> k p", p=P), consts_in)
            load(x[:, 0, :], ins["x_prompt"][0], consts_in)
            load(x[:, 1:3, :], ins["x_sample"][0].rearrange("(b p) d -> p b d", p=P), consts_in)
            for t, name in ((dftL, "const_dft_latent"), (dftP, "const_dft_prompt"), (dftC, "const_dft_channel"),
                            (poolL, "const_pool_latent"), (poolP, "const_pool_prompt"), (rope, "const_rope"),
                            (na_mask, "const_na_mask")):
                load(t[:], ins[name], consts_in)
            load_small(0)
            load_ln(0, 1, ln1_in)
            act.wait_ge(consts_in, 16 * 12)
            act.wait_ge(pool_ready, 1)

            st.take(turn_ready)
            st.step(nc.scalar.activation(silu_c[:], ps_turn[:, 0:2 * KC].rearrange("p (s k) -> p s k", s=2),
                                         ACT.Silu), turn_free)

            def root(l_sem_in, out, in_, scale, l_sem_out):
                st.take(l_sem_in)
                st.give(nc.scalar.activation(out, in_, ACT.Sqrt, bias=eps[:], scale=scale), l_sem_out)

            def modulate(b, sh, sc):
                st.take(turn_ready)
                for k in range(KC):
                    ins_ = nc.scalar.activation(hT[:, k, b * P:(b + 1) * P], ps_turn[:, k * P:(k + 1) * P], ACT.Identity,
                                                bias=ada[:, sh + k, stream(b):stream(b) + 1],
                                                scale=ada[:, sc + k, stream(b):stream(b) + 1])
                st.step(ins_, turn_free)
                act.sem_inc(hT_ready, 1)

            def gates():
                for s in range(2):
                    st.take(turn_ready)
                    ins_ = nc.scalar.copy(gate[:, s, :], ps_turn)
                    st.step(ins_, turn_free)
                act.sem_inc(gate_ready, 1)

            for l in range(DEPTH):
                st.take(proj_ready)
                st.step(nc.scalar.copy(ada_raw[:], ps_proj[st.taken["proj_ready"] % 2 ^ 1][:, 0:146]), proj_free)
                act.sem_inc(ada_raw_ready, 1)
                st.take(ada_ready)
                if l > 0:
                    act.wait_ge(gate_used, l * 2)
                gates()
                for b in range(NB):
                    root(var_ready, std[:], mv[:, 1:2], 1.0, std_ready)
                    modulate(b, SH1, SC1)

                def evacuate(*pairs, scale=1.0):
                    st.take(proj_ready)
                    src = ps_proj[st.taken["proj_ready"] % 2 ^ 1]
                    for dst, lo, hi in pairs:
                        ins_ = nc.scalar.activation(dst, src[:, lo:hi], ACT.Copy, scale=scale)
                    st.step(ins_, proj_free)
                    act.sem_inc(in_ready, 1)

                if l > 0:
                    act.wait_ge(out_done, 32 * l)
                for j in range(IN_T):
                    if j in (T_NQ, T_NK):
                        for c in range(2):
                            evacuate(((nqT if j == T_NQ else nkT)[:, c, 0:T], 0, T), scale=0.125 if j == T_NQ else 1.0)
                        continue
                    for b in range(NB):
                        if j == T_AQ:
                            evacuate((qk[:, b, 0:4, :].rearrange("p h d -> p (h d)"), 0, 256))
                        elif j == T_AKV:
                            evacuate((qk[:, b, 4:6, :].rearrange("p h d -> p (h d)"), 0, 128), (av[:, b, :], 128, 256))
                        else:
                            evacuate(({T_FX: fx, T_NV: nv, T_PX: px}[j][:, b, :], 0, 256))
                act.dma_start(outs[3][0, l].rearrange("t h d -> t (h d)"), av[:, 0, :]).then_inc(out_done, 16)
                act.dma_start(outs[5][0, l].rearrange("t h d -> t (h d)"), nv[:, 0, :]).then_inc(out_done, 16)

                st.take(turn_ready)
                nc.scalar.copy(akT[:, T:KEYS], ps_turn[:, 0:P])
                nc.scalar.copy(nkT[:, :, T:KEYS], ps_turn[:, P:3 * P].rearrange("p (c n) -> p c n", c=2))
                nc.scalar.copy(k12T[:], ps_turn[:, 512:512 + 2 * P].rearrange("p (c n) -> p c n", c=2))
                if l > 0:
                    act.wait_ge(k_out_done, 32 * l)
                st.step(nc.scalar.copy(nk_out[:], ps_turn[:, 768:1024]), turn_free)
                act.sem_inc(att_in_ready, 1)
                act.dma_start(outs[4][0, l].rearrange("t h d -> t (h d)"), nk_out[:]).then_inc(k_out_done, 16)

                for b in range(NB):
                    root(ss_ready, ss2[:], ss[:], 1.0 / HD, srt_ready)
                    if b == 0:
                        act.wait_ge(k_out_ready, l + 1)
                        act.dma_start(outs[2][0, l].rearrange("t h d -> t (h d)"),
                                      qkn[:, 4:6, :].rearrange("p h d -> p (h d)")).then_inc(k_out_done, 16)
                    st.take(turn_ready)
                    nc.scalar.activation(aqT[:, :, b * P:(b + 1) * P], ps_turn[:, 0:2 * P].rearrange("p (c n) -> p c n", c=2),
                                         ACT.Copy, scale=0.125)
                    st.step(nc.scalar.copy(akT[:, b * P:(b + 1) * P], ps_turn[:, 2 * P:3 * P]), turn_free)
                    act.sem_inc(att_in_ready, 1)

                def side(dst, lo, hi, plo=0, phi=P, scale=1.0, final=False):
                    st.take(proj_ready)
                    src = ps_proj[st.taken["proj_ready"] % 2 ^ 1]
                    st.step(nc.scalar.activation(dst, src[plo:phi, lo:hi], ACT.Copy, scale=scale), proj_free)
                    act.sem_inc(mix_side_ready if final else side_ready, 1)

                for c in range(2):
                    for m in range(2):
                        side(dT[:, c, m, :], 0, T)
                for c in range(2):
                    side(yT[:, c, :], 0, T)
                for c in range(2):
                    side(poolT[:, c, :], 0, T)
                for c in range(2):
                    side(mixT[:, 2 + c, :], 0, T, final=True)
                for c in range(2):
                    side(mixT[:, 6 + c, :], 0, T, scale=p_scale[:, c:c + 1], final=True)

                def exponent(n):
                    b, m, h = JOBS[n]
                    w = KEY_HI[b] - KEY_LO[b]
                    st.take(nmax_ready)
                    if n >= 2:
                        act.wait_ge(pt_ready, l * len(JOBS) + n - 1)
                    src = score[:, n % 2, :] if (m and b) else ps_sc[n % 2]
                    st.step(nc.scalar.activation(prob[:, n % 2, 0:w], src[:, 0:w], ACT.Exp, bias=nmax[:, n % 2:n % 2 + 1],
                                                 accum_out=psums[:, n % 2:n % 2 + 1]), exp_ready)

                def head_out(n):
                    if n % 2:
                        b, m, h = JOBS[n]
                        act.wait_ge(o_ready, l * len(JOBS) + n + 1)
                        st.step(nc.scalar.copy(mixT[:, (4 if m else 0) + h // 2, b * P:(b + 1) * P], ps_o[:, 0:P]), o_free)

                for n in range(len(JOBS)):
                    exponent(n)
                    if n >= 2:
                        head_out(n - 2)
                head_out(len(JOBS) - 2)
                head_out(len(JOBS) - 1)

                for b in range(NB):
                    root(var_ready, std[:], mv[:, 1:2], 1.0, std_ready)
                act.wait_ge(ln1_used, l + 1)
                load_ln(l, 2, ln2_in)
                act.wait_ge(gate_used, 2 * l + 1)
                gates()
                for b in range(NB):
                    root(var_ready, std[:], mv[:, 1:2], 1.0, std_ready)
                    modulate(b, SH2, SC2)
                    st.take(turn_ready)
                    st.step(nc.scalar.copy(h2[:, b, :], ps_turn), turn_free)
                    act.sem_inc(h2_ready, 1)
                for j in range(Q_T):
                    for half in range(2):
                        st.take(proj_ready)
                        if j > 0:
                            act.wait_ge(top_ready, l * Q_T + j)
                        st.step(nc.scalar.copy(qT[:, half, :], ps_proj[st.taken["proj_ready"] % 2 ^ 1][:, 0:T]), proj_free)
                        act.sem_inc(qT_ready, 1)
                if l + 1 < DEPTH:
                    st.take(small_used)
                    load_small(l + 1)
                for b in range(NB):
                    step = l * NB + b
                    st.take(gexp_in)
                    st.give(nc.scalar.activation(gw[:], gw[:], ACT.Exp), gexp_out)

                    def group(base, g):
                        first = step * PICKS + base * (BODY * GROUP) + g * GROUP
                        turn = step * (PICKS // GROUP) + base * BODY + g
                        act.wait_ge(u_free, first + GROUP + SLOTS)
                        nc.scalar.activation(gelu[:], dots[:], ACT.Gelu).then_inc(gelu_ready, 1)
                        act.wait_ge(weight_ready, turn + 1)
                        for m in range(GROUP):
                            act.wait_ge(v_free, first + m + 1)
                            nc.scalar.activation(diag[:, m, :], ident[:], ACT.Copy,
                                                 scale=weight[:, m:m + 1]).then_inc(diag_ready, 1)

                    with act.Fori(0, PICKS // (BODY * GROUP)) as i:
                        for g in range(BODY):
                            group(i, g)
                    root(var_ready, std[:], mv[:, 1:2], 1.0, std_ready)
                    if l + 1 == DEPTH:
                        act.wait_ge(x_ready, l * NB + b + 1)
                        dst = outs[0][0] if b == 0 else outs[1][0, (b - 1) * P:b * P, :]
                        act.dma_start(dst, x[:, b, :]).then_inc(out_done, 16)
                if l + 1 < DEPTH:
                    act.wait_ge(ln2_used, l + 1)
                    load_ln(l + 1, 1, ln1_in)
            act.wait_ge(out_done, 16 * (2 * DEPTH + NB))
            act.wait_ge(k_out_done, 32 * DEPTH)

        @block.vector
        def _(dve):
            st = Steps(dve)
            V = nc.vector

            def step(ins_):
                st.step(ins_, dve_step)

            dve.wait_ge(consts_in, 16 * 12)
            dve.wait_ge(pool_ready, 1)

            def norm_stats(b):
                V.bn_stats(stats[:, 0, :], x[:, b, 0:512])
                step(V.bn_stats(stats[:, 1, :], x[:, b, 512:1024]))
                st.step(V.bn_aggr(mv[:], stats[:].rearrange("p a b -> p (a b)")), var_ready)
                st.take(std_ready)
                step(V.reciprocal(rstd[:], std[:]))

            def normalize(dst, b):
                return V.tensor_scalar(dst, x[:, b, :], mv[:, 0:1], rstd[:], ALU.subtract, ALU.mult)

            def post_norm(b, final):
                norm_stats(b)
                step(normalize(x[:, b, :], b))
                step(V.tensor_tensor(x[:, b, :], x[:, b, :], ln_g[:], ALU.mult))
                st.step(V.tensor_tensor(x[:, b, :], x[:, b, :], ln_b[:], ALU.add), final)

            for l in range(DEPTH):
                st.take(small_in, 1, 16 * 35)
                st.take(ada_raw_ready)
                step(V.tensor_tensor(ada[:], ada_raw[:, 0:96].rearrange("p (c s) -> p c s", s=2),
                                     ada_raw[:, 96:144].unsqueeze(2).to_broadcast([P, 6 * KC, 2]), ALU.add))
                V.tensor_scalar(ada[:, SC1:SC1 + KC, :], ada[:, SC1:SC1 + KC, :], 1.0, None, ALU.add)
                st.step(V.tensor_scalar(ada[:, SC2:SC2 + KC, :], ada[:, SC2:SC2 + KC, :], 1.0, None, ALU.add), ada_ready)

                for b in range(NB):
                    norm_stats(b)
                    if b > 0:
                        dve.wait_ge(turn_ready, turn_at(l, "ln1", b - 1))
                    st.step(normalize(xhat[:], b), xhat_ready)

                dve.wait_ge(in_ready, in_at(l, T_AKV, NB - 1))
                for b in range(NB):
                    step(V.tensor_tensor(sq[:], qk[:, b], qk[:, b], ALU.mult))
                    st.step(V.tensor_reduce(ss[:], sq[:], AX_X, ALU.add), ss_ready)
                    st.take(srt_ready)
                    step(V.reciprocal(ss[:], ss2[:]))
                    step(V.tensor_tensor(sq[:], qk[:, b], ss[:].unsqueeze(2).to_broadcast([P, 6, HD]), ALU.mult))
                    if b > 0:
                        dve.wait_ge(turn_ready, turn_at(l, "qk", b - 1))
                    if b == 1:
                        dve.wait_ge(k_out_done, 32 * (l + 1))
                    step(V.tensor_tensor(sq[:], sq[:], qk_g[:], ALU.mult))
                    if b == 0:
                        V.tensor_copy(qkn[:, 0:4, :].rearrange("p (g k) d -> p k g d", g=2),
                                      sq[:, 0:4, :].rearrange("p (k g) d -> p k g d", g=2))
                        st.step(V.tensor_copy(qkn[:, 4:6, :], sq[:, 4:6, :]), k_out_ready)
                        dve.sem_inc(qkn_ready, 1)
                        continue
                    cos = rope[:, b - 1, 0, :].unsqueeze(1).to_broadcast([P, 6, HD])
                    r5 = rot[:].rearrange("p h (e d) -> p h e d", e=4)
                    s5 = sq[:].rearrange("p h (e d) -> p h e d", e=4)
                    sin = rope[:, b - 1, 1, :].rearrange("p (e d) -> p e d", e=4)
                    for e in range(4):
                        ins_ = V.tensor_tensor(r5[:, :, e, :], s5[:, :, e ^ 1, :],
                                               sin[:, e, :].unsqueeze(1).to_broadcast([P, 6, 16]), ALU.mult)
                    step(ins_)
                    step(V.tensor_tensor(sq[:], sq[:], cos, ALU.mult))
                    V.tensor_tensor(qkn[:, 0:4, :].rearrange("p (g k) d -> p k g d", g=2),
                                    sq[:, 0:4, :].rearrange("p (k g) d -> p k g d", g=2),
                                    rot[:, 0:4, :].rearrange("p (k g) d -> p k g d", g=2), ALU.add)
                    step(V.tensor_tensor(qkn[:, 4:6, :], sq[:, 4:6, :], rot[:, 4:6, :], ALU.add))
                    dve.sem_inc(qkn_ready, 1)

                st.take(bias_ready)
                J = len(JOBS)

                def maximum(n):
                    b, m, h = JOBS[n]
                    w = KEY_HI[b] - KEY_LO[b]
                    st.take(s_ready)
                    src = ps_sc[n % 2][:, 0:w]
                    if m and b:
                        step(V.tensor_tensor(score[:, n % 2, 0:w], src, na_b[:, b - 1, h, :], ALU.add))
                        src = score[:, n % 2, 0:w]
                    st.step(V.tensor_reduce(nmax[:, n % 2:n % 2 + 1], src, AX_X, ALU.max, negate=True), nmax_ready)

                def divide(n):
                    b, m, h = JOBS[n]
                    w = KEY_HI[b] - KEY_LO[b]
                    st.take(exp_ready)
                    step(V.reciprocal(pinv[:, n % 2:n % 2 + 1], psums[:, n % 2:n % 2 + 1]))
                    st.step(V.tensor_scalar(prob[:, n % 2, 0:w], prob[:, n % 2, 0:w], pinv[:, n % 2:n % 2 + 1], None,
                                            ALU.mult), prob_ready)

                def copy_t(n):
                    b, m, h = JOBS[n]
                    w = KEY_HI[b] - KEY_LO[b]
                    st.take(pt_ready)
                    if n >= 2:
                        dve.wait_ge(o_ready, l * J + n - 1)
                    st.step(V.tensor_copy(probT[:, n % 2, 0:w], ps_pt[:, 0:w]), probT_ready)

                maximum(0)
                for n in range(J):
                    if n + 1 < J:
                        maximum(n + 1)
                    divide(n)
                    if n >= 1:
                        copy_t(n - 1)
                copy_t(J - 1)

                st.take(gate_ready)
                dve.wait_ge(turn_ready, turn_at(l, "ln1", NB - 1))
                for j in range(OUT_T):
                    for b in range(NB):
                        c = slice(j * WT, (j + 1) * WT)
                        st.take(mo_ready)
                        st.step(V.tensor_tensor(xhat[:, c], ps_sc[(j * NB + b) % 2][:, 0:WT], gate[:, stream(b), c], ALU.mult), mo_free)
                        step(V.scalar_tensor_tensor(x[:, b, c], x[:, b, c], ALPHA, xhat[:, c], ALU.mult, ALU.add))
                dve.sem_inc(gate_used, 1)
                st.take(ln1_in, 2, 16)
                for b in range(NB):
                    post_norm(b, dve_step)
                dve.sem_inc(ln1_used, 1)
                st.take(gate_ready)
                for b in range(NB):
                    norm_stats(b)
                    if b > 0:
                        dve.wait_ge(turn_ready, turn_at(l, "ln2", b - 1))
                    else:
                        dve.wait_ge(turn_ready, turn_at(l, "ln1", NB - 1))
                    st.step(normalize(xhat[:], b), xhat_ready)

                for j in range(Q_T):
                    st.take(top_ready)
                    pick = [(b, half) for b in range(NB) for half in range(2)]
                    src = [ps_top[:, i * P:(i + 1) * P] for i in range(6)]
                    for i, (b, half) in enumerate(pick):
                        ins_ = V.max(best[:, b, half, j, 0:8], src[i])
                    step(ins_)
                    for i, (b, half) in enumerate(pick):
                        V.max_index(best_i[:, b, half, j, 0:8], best[:, b, half, j, 0:8], src[i])
                        ins_ = V.match_replace(scr[:, i, :], best[:, b, half, j, 0:8], src[i], LOW)
                    st.step(ins_, top_free)
                    for i, (b, half) in enumerate(pick):
                        ins_ = V.max(best[:, b, half, j, 8:16], scr[:, i, :])
                    step(ins_)
                    for i, (b, half) in enumerate(pick):
                        ins_ = V.max_index(best_i[:, b, half, j, 8:16], best[:, b, half, j, 8:16], scr[:, i, :])
                    step(ins_)

                st.take(ln2_in, 2, 16)
                for b in range(NB):
                    turn = l * NB + b
                    step(V.tensor_tensor(cand[:].rearrange("p h (i j) -> p h i j", i=TOPK),
                                         best[:, b, 0].unsqueeze(3).to_broadcast([P, HEADS, TOPK, TOPK]),
                                         best[:, b, 1].unsqueeze(2).to_broadcast([P, HEADS, TOPK, TOPK]), ALU.add))
                    for h in range(HEADS):
                        ins_ = V.max(top[:, h, 0:8], cand[:, h, :])
                    step(ins_)
                    for h in range(HEADS):
                        V.max_index(pos[:, h, 0:8], top[:, h, 0:8], cand[:, h, :])
                        ins_ = V.match_replace(cand2[:, h, :], top[:, h, 0:8], cand[:, h, :], LOW)
                    step(ins_)
                    for h in range(HEADS):
                        ins_ = V.max(top[:, h, 8:16], cand2[:, h, :])
                    step(ins_)
                    st.step(V.tensor_tensor(gw[:], top[:], top[:, :, 0:1].to_broadcast([P, HEADS, TOPK]), ALU.subtract), gexp_in)
                    for h in range(HEADS):
                        ins_ = V.max_index(pos[:, h, 8:16], top[:, h, 8:16], cand2[:, h, :])
                    step(ins_)
                    V.tensor_scalar(pos_ij[:, 0], pos[:], 4, None, ALU.logical_shift_right)
                    step(V.tensor_scalar(pos_ij[:, 1], pos[:], 15, None, ALU.bitwise_and))
                    V.tensor_copy(pos_f[:], pos_ij[:])
                    step(V.tensor_copy(best_f[:], best_i[:, b]))
                    for half in range(2):
                        c4 = cand[:].rearrange("p h (k i) -> p h k i", k=TOPK)
                        c5 = cand2[:].rearrange("p h (k i) -> p h k i", k=TOPK)
                        step(V.tensor_tensor(c4, pos_f[:, half].unsqueeze(3).to_broadcast([P, HEADS, TOPK, TOPK]),
                                             iota16[:].unsqueeze(1).unsqueeze(1).to_broadcast([P, HEADS, TOPK, TOPK]), ALU.is_equal))
                        step(V.tensor_tensor(c5, c4, best_f[:, half].unsqueeze(2).to_broadcast([P, HEADS, TOPK, TOPK]), ALU.mult))
                        step(V.tensor_reduce(found[:, half], c5, AX_X, ALU.add))
                    step(V.tensor_scalar(idx_f[:].rearrange("p (h k) -> p h k", h=HEADS), found[:, 0], float(N_KEYS),
                                         float(l * EXPERTS), ALU.mult, ALU.add))
                    st.step(V.tensor_tensor(idx[:].rearrange("p (h k) -> p h k", h=HEADS),
                                            idx_f[:].rearrange("p (h k) -> p h k", h=HEADS), found[:, 1], ALU.add), idx_ready)
                    st.take(gexp_out)
                    step(V.tensor_reduce(gsum[:], gw[:], AX_X, ALU.add))
                    step(V.reciprocal(gsum[:], gsum[:]))
                    step(V.tensor_tensor(gw[:], gw[:], gsum[:].unsqueeze(2).to_broadcast([P, HEADS, TOPK]), ALU.mult))
                    if b == 0:
                        st.take(h2_ready, NB)

                    gflat = gw[:].rearrange("p h k -> p (h k)")

                    def group(base, g):
                        first = turn * PICKS + base * (BODY * GROUP) + g * GROUP
                        for m in range(GROUP):
                            row = turn * (PICKS // SLOTS) + base * BODY + g
                            dve.wait_ge(u_landed[m], (row + 1) * 16)
                            dve.wait_ge(u_free, first + m + SLOTS)
                            V.tensor_tensor_reduce(out=junk[:], in0=u_rows[:, m, :], in1=h2[:, b, :], scale=1.0, scalar=0.0,
                                                   op0=ALU.mult, op1=ALU.add, accum_out=dots[:, m:m + 1]).then_inc(u_free, 1)
                        dve.wait_ge(gelu_ready, turn * (PICKS // GROUP) + base * BODY + g + 1)
                        at_ = bass.ds(base * (BODY * GROUP) + g * GROUP, GROUP)
                        V.tensor_tensor(weight[:], gelu[:], gflat[:, at_], ALU.mult).then_inc(weight_ready, 1)
                        dve.wait_ge(weight_ready, turn * (PICKS // GROUP) + base * BODY + g + 1)

                    with dve.Fori(0, PICKS // (BODY * GROUP)) as i:
                        for g in range(BODY):
                            group(i, g)
                    dve.wait_ge(u_free, (turn + 1) * PICKS + SLOTS)
                    dve.wait_ge(v_free, (turn + 1) * PICKS + SLOTS)
                    st.step(V.tensor_tensor(junk[:], ps_y, gate[:, stream(b), :], ALU.mult), y_free)
                    step(V.scalar_tensor_tensor(x[:, b, :], x[:, b, :], ALPHA, junk[:], ALU.mult, ALU.add))
                    post_norm(b, x_ready)
                dve.sem_inc(gate_used, 1)
                dve.sem_inc(ln2_used, 1)

        @block.tensor
        def _(pe):
            st = Steps(pe)
            M = nc.tensor

            zero_by = dftL[:].rearrange("p m k n -> p (m k n)")
            tiles = [0]

            def weights():
                n = tiles[0]
                tiles[0] += 1
                pe.wait_ge(w_landed[n % RING], 16 * (n // RING + 1))
                return ring[:, n % RING]

            projs = [0]

            def proj():
                st.free(proj_free, 2)
                projs[0] += 1
                return ps_proj[(projs[0] - 1) % 2]

            def turn_in():
                st.free(turn_free, 1)

            pe.wait_ge(consts_in, 16 * 12)
            pe.wait_ge(pool_ready, 1)
            turn_in()
            st.give(M.transpose(ps_turn[:, 0:2 * KC], crow[:], ident[0:2 * KC, 0:2 * KC]), turn_ready)
            pe.wait_ge(turn_free, 1)

            def transposes(give):
                for k in range(KC):
                    ins_ = M.transpose(ps_turn[:, k * P:(k + 1) * P], xhat[:, k * P:(k + 1) * P], ident[:])
                st.give(ins_, turn_ready)

            def gates(g):
                for s in range(2):
                    turn_in()
                    for k in range(KC):
                        ins_ = M.matmul(ps_turn[:, k * P:(k + 1) * P], ada[:, g + k, s:s + 1].to_broadcast([P, P]), ident[:],
                                        start=True, stop=True)
                    st.give(ins_, turn_ready)

            for l in range(DEPTH):
                J = len(JOBS)
                pe.wait_ge(small_in, 16 * 35 * (l + 1))
                out = proj()
                for j in range(ADA_T):
                    w = weights()
                    for m in range(2):
                        for k in range(KC):
                            ins_ = M.matmul(out[:, 4 * j + 2 * m:4 * j + 2 * m + 2], w[:, k, m * P:(m + 1) * P], silu_c[:, :, k],
                                            start=(k == 0), stop=(k == KC - 1))
                    st.give(ins_, w_used)
                st.give(M.transpose(out[:, 96:146], b_row[:], ident[0:6 * KC + 2, 0:6 * KC + 2]), proj_ready)
                st.take(ada_ready)
                if l > 0:
                    pe.wait_ge(y_free, NB * l)
                gates(G1)
                for b in range(NB):
                    st.take(xhat_ready)
                    turn_in()
                    transposes(turn_ready)

                st.take(hT_ready, NB)
                for j in range(IN_T):
                    w = weights()
                    if j in (T_NQ, T_NK):
                        for c in range(2):
                            out = proj()
                            for k in range(KC):
                                ins_ = M.matmul(out[:, 0:T], w[:, k, c * P:(c + 1) * P], hT[:, k, :], start=(k == 0), stop=(k == KC - 1))
                            if c == 0:
                                st.give(ins_, proj_ready)
                    else:
                        for b in range(NB):
                            out = proj()
                            for k in range(KC):
                                ins_ = M.matmul(out[:, 0:WT], hT[:, k, b * P:(b + 1) * P], w[:, k, :], start=(k == 0), stop=(k == KC - 1))
                            if b < NB - 1:
                                st.give(ins_, proj_ready)
                    st.give(ins_, proj_ready)
                    pe.wait_ge(proj_ready, st.given["proj_ready"])
                    pe.sem_inc(w_used, 1)

                pe.wait_ge(in_ready, in_at(l, T_PX, NB - 1))
                turn_in()
                for c in range(3):
                    M.transpose(ps_turn[:, c * P:(c + 1) * P], cache_k[:, c * P:(c + 1) * P], ident[:])
                for c in range(2):
                    M.transpose(ps_turn[:, 512 + c * P:512 + (c + 1) * P], k12[:, c, :], ident[:])
                for c in range(2):
                    ins_ = M.transpose(ps_turn[:, 768 + c * P:768 + (c + 1) * P], nkT[:, c, 0:P], ident[:])
                st.give(ins_, turn_ready)
                for b in range(NB):
                    st.take(qkn_ready)
                    turn_in()
                    for g in range(3):
                        ins_ = M.transpose(ps_turn[:, g * P:(g + 1) * P], qkn[:, 2 * g:2 * g + 2, :].rearrange("p h d -> p (h d)"), ident[:])
                    st.give(ins_, turn_ready)

                for c in range(2):
                    for m in range(2):
                        out = proj()
                        cc = slice(c * P, (c + 1) * P)
                        M.matmul(out[:, 0:P], fx[:, 0, cc], dftP[:, m, :], start=True, stop=True)
                        for k in range(2):
                            ins_ = M.matmul(out[:, P:T], fx[:, 1 + k, cc], dftL[:, m, k, :], start=(k == 0), stop=(k == 1))
                        st.give(ins_, proj_ready)
                st.take(side_ready, 4)
                for c in range(2):
                    out = proj()
                    for m in range(2):
                        ins_ = M.matmul(out[:, 0:T], dftC[:, m, :], dT[:, c, m, :], start=(m == 0), stop=(m == 1))
                    st.give(ins_, proj_ready)
                for c in range(2):
                    out = proj()
                    for g in (2 * c, 2 * c + 1):
                        lo, cc = 64 * (g % 2), slice(g * HD, (g + 1) * HD)
                        M.matmul(out[lo:lo + 64, 0:P], px[:, 0, cc], poolP[:, g, :], start=True, stop=True)
                        for k in range(2):
                            ins_ = M.matmul(out[lo:lo + 64, P:T], px[:, 1 + k, cc], poolL[:, g, k, :], start=(k == 0), stop=(k == 1))
                    st.give(ins_, proj_ready)
                st.take(side_ready, 2)
                for c in range(2):
                    out = proj()
                    for k in range(2):
                        ins_ = M.matmul(out[:, 0:T], wf[:, k, c * P:(c + 1) * P], yT[:, k, :], start=(k == 0), stop=(k == 1))
                    st.give(ins_, proj_ready)
                st.take(side_ready, 2)
                for c in range(2):
                    out = proj()
                    for lo in (0, 64):
                        ins_ = M.matmul(out[lo:lo + 64, 0:T], wp[lo:lo + 64, c, :], poolT[lo:lo + 64, c, :], start=True, stop=True)
                    st.give(ins_, proj_ready)

                pe.wait_ge(att_in_ready, (l + 1) * (1 + NB))

                def scores(n):
                    b, m, h = JOBS[n]
                    lo, hi = KEY_LO[b], KEY_HI[b]
                    q, keys = (nqT, nkT[:, h // 2, :]) if m else (aqT, akT)
                    r, c = (h % 2, h // 2) if m else (h // 2, h % 2)
                    if n >= 2:
                        pe.wait_ge(exp_ready, l * J + n - 1)
                    st.give(M.matmul(ps_sc[n % 2][:, 0:hi - lo], q[64 * r:64 * r + 64, c, b * P:(b + 1) * P],
                                     keys[64 * r:64 * r + 64, lo:hi], start=True, stop=True), s_ready)

                def turn_probs(n):
                    b, m, h = JOBS[n]
                    st.take(prob_ready)
                    if n >= 1:
                        pe.wait_ge(probT_ready, l * J + n)
                    for k in range((KEY_HI[b] - KEY_LO[b]) // P):
                        ins_ = M.transpose(ps_pt[:, k * P:(k + 1) * P], prob[:, n % 2, k * P:(k + 1) * P], ident[:])
                    st.give(ins_, pt_ready)

                def values(n):
                    b, m, h = JOBS[n]
                    st.take(probT_ready)
                    if n % 2 == 0:
                        st.free(o_free, 1)
                    nk = (KEY_HI[b] - KEY_LO[b]) // P
                    lo = 64 * (h % 2)
                    v = nv[:, :, h * HD:(h + 1) * HD] if m else av[:, :, (h // 2) * HD:(h // 2 + 1) * HD]
                    for k in range(nk):
                        ins_ = M.matmul(ps_o[lo:lo + 64, 0:P], v[:, KEY_LO[b] // P + k, :], probT[:, n % 2, k * P:(k + 1) * P],
                                        start=(k == 0), stop=(k == nk - 1))
                    st.give(ins_, o_ready)

                scores(0)
                for n in range(J):
                    if n + 1 < J:
                        scores(n + 1)
                    turn_probs(n)
                    if n >= 1:
                        values(n - 1)
                values(J - 1)

                st.take(mix_side_ready, 4)
                pe.wait_ge(o_free, (l + 1) * J // 2)
                for j in range(OUT_T):
                    w = weights()
                    for b in range(NB):
                        st.free(mo_free, 2)
                        for k in range(KC):
                            ins_ = M.matmul(ps_sc[(j * NB + b) % 2][:, 0:WT], mixT[:, k, b * P:(b + 1) * P], w[:, k, :],
                                            start=(k == 0), stop=(k == KC - 1))
                        st.give(ins_, mo_ready)
                    pe.wait_ge(mo_ready, st.given["mo_ready"])
                    pe.sem_inc(w_used, 1)
                gates(G2)
                for b in range(NB):
                    st.take(xhat_ready)
                    turn_in()
                    transposes(turn_ready)
                    st.take(hT_ready)
                    turn_in()
                    for k in range(KC):
                        ins_ = M.transpose(ps_turn[:, k * P:(k + 1) * P], hT[:, k, b * P:(b + 1) * P], ident[:])
                    st.give(ins_, turn_ready)
                for j in range(Q_T):
                    w = weights()
                    for half in range(2):
                        out = proj()
                        for k in range(KC):
                            ins_ = M.matmul(out[:, 0:T], w[:, k, half * P:(half + 1) * P], hT[:, k, :], start=(k == 0), stop=(k == KC - 1))
                        st.give(ins_, proj_ready)
                    pe.wait_ge(proj_ready, st.given["proj_ready"])
                    pe.sem_inc(w_used, 1)
                    st.take(qT_ready, 2)
                    if j == 0:
                        pe.wait_ge(mo_free, (l + 1) * OUT_T * NB)
                    st.free(top_free, 1)
                    for b in range(NB):
                        for half in range(2):
                            i = b * 2 + half
                            ins_ = M.matmul(ps_top[:, i * P:(i + 1) * P], qT[:, half, b * P:(b + 1) * P], k12T[:, half, :],
                                            start=True, stop=True)
                    st.give(ins_, top_ready)
                pe.wait_ge(top_ready, (l + 1) * Q_T)
                pe.sem_inc(small_used, 1)
                for b in range(NB):
                    turn = l * NB + b
                    if b == 0:
                        pe.wait_ge(turn_free, turn_at(l, "back", NB - 1))
                    st.free(y_free, 1)
                    for half in range(2):
                        ins_ = M.matmul(ps_y[:, half * 512:(half + 1) * 512], zeros[:], zero_by[:, half * 512:(half + 1) * 512], start=True, stop=True,
                                        skip_group_check=True)

                    def group(base, g):
                        first = turn * PICKS + base * (BODY * GROUP) + g * GROUP
                        for m in range(GROUP):
                            pe.wait_ge(diag_ready, first + m + 1)
                            pe.wait_ge(v_landed[m], (turn * (PICKS // SLOTS) + base * BODY + g + 1) * 16)
                            for half in range(2):
                                ins_ = M.matmul(ps_y[:, half * 512:(half + 1) * 512], diag[:, m, :],
                                                v_rows[:, m, half * 512:(half + 1) * 512], start=False, stop=True,
                                                skip_group_check=True)
                            ins_.then_inc(v_free, 1)

                    with pe.Fori(0, PICKS // (BODY * GROUP)) as i:
                        for g in range(BODY):
                            group(i, g)


_INS = ["x_prompt", "x_sample", "cache_attn_k", "cache_attn_v", "cache_na_k", "cache_na_v", "c", "c_ctx", "w_ada", "b_ada",
        "w_in", "q_norm_g", "k_norm_g", "w_fourier", "w_pool", "pool_scale", "w_out", "ln1_g", "ln1_b",
        "ln2_g", "ln2_b", "peer_wq", "peer_k1", "peer_k2", "peer_u", "peer_v"]
_OUTS = [(1, 128, 1024), (1, 256, 1024), (1, 2, 128, 2, 64), (1, 2, 128, 2, 64), (1, 2, 128, 4, 64), (1, 2, 128, 4, 64)]


def constants():
    import numpy as np

    def dft(n):
        a = 2 * np.pi * (np.outer(np.arange(n), np.arange(n)) % n) / n
        return np.cos(a), np.sin(a)

    out = {"const_ident": np.eye(P)}
    c, s = (t / np.sqrt(2 * P * HD) for t in dft(2 * P))
    out["const_dft_latent"] = np.stack([c, s]).reshape(2, 2, P, 2 * P).transpose(2, 0, 1, 3)
    c, s = (t / np.sqrt(P * HD) for t in dft(P))
    out["const_dft_prompt"] = np.stack([c, s]).transpose(1, 0, 2)
    c, s = dft(HD)
    out["const_dft_channel"] = np.stack([np.kron(np.eye(2), c), np.kron(np.eye(2), -s)]).transpose(1, 0, 2)

    def pool(n):
        m = np.zeros((4, n, n))
        for g, w in enumerate((2, 4, 8, 16)):
            for t in range(n):
                lo, hi = np.clip([t - w // 2, t - w // 2 + w], 0, n)
                m[g, lo:hi, t] = 1.0 / (hi - lo)
                m[g, t, t] -= 1.0
        return m

    out["const_pool_latent"] = pool(2 * P).reshape(4, 2, P, 2 * P).transpose(2, 0, 1, 3)
    out["const_pool_prompt"] = pool(P).transpose(1, 0, 2)
    t = np.arange(2 * P)
    nf = HD // 4
    inv = 10000.0 ** (-np.arange(nf) / nf)
    cos, sin = [], []
    for at in (t // GRID_W, t % GRID_W):
        ang = at[:, None] * inv[None, :]
        cos += [np.cos(ang)] * 2
        sin += [-np.sin(ang), np.sin(ang)]
    out["const_rope"] = np.stack([np.concatenate(cos, -1), np.concatenate(sin, -1)], 1).reshape(2, P, 2, HD).transpose(1, 0, 2, 3)
    col = np.arange(2 * P) % GRID_W
    first = np.clip(col - NA_KW // 2, 0, GRID_W - NA_KW)
    seen = (col[None, :] >= first[:, None]) & (col[None, :] < first[:, None] + NA_KW)
    out["const_na_mask"] = np.where(seen, 0.0, -1e30).reshape(2, P, 2 * P).transpose(1, 0, 2)
    return {k: np.ascontiguousarray(v.astype(np.float32)) for k, v in out.items()}


def slide(table):
    import numpy as np

    off = GRID_W - NA_KW
    wide = np.pad(table, ((0, 0), (0, 0), (0, 0), (off, off)))
    return np.stack([wide[..., GRID_W - 1 - qc:2 * GRID_W - 1 - qc] for qc in range(GRID_W)], axis=2)


def kernel(**inputs):
    import numpy as _np
    import concourse.bacc as _bacc
    from concourse import mybir as _mybir
    from concourse.bass_utils import run_bass_kernel_spmd as _run

    nc = _bacc.Bacc("TRN2", target_bir_lowering=False, num_devices=1)
    arrays, args = {}, {}
    laid_out = [("na_bias_slid", slide(_np.asarray(inputs["na_bias"])))]
    for name, a in [(n, inputs[n]) for n in _INS] + laid_out + list(constants().items()):
        a = _np.ascontiguousarray(a)
        arrays[f"in_{name}_dram"] = a
        args[name] = nc.dram_tensor(f"in_{name}_dram", a.shape, _mybir.dt.from_np(a.dtype), kind="ExternalInput").ap()
    outs = [nc.dram_tensor(f"out_{i}_dram", shape, _mybir.dt.float32, kind="ExternalOutput").ap()
            for i, shape in enumerate(_OUTS)]
    program(nc, args, outs)
    r = _run(nc, [arrays], core_ids=[0])
    return tuple(r.results[0][f"out_{i}_dram"] for i in range(len(_OUTS)))
```

```python
from contextlib import ExitStack

import concourse.bass as bass
from concourse import mybir

F32 = mybir.dt.float32
U32 = mybir.dt.uint32
ALU = mybir.AluOpType
ACT = mybir.ActivationFunctionType
AX_X = mybir.AxisListType.X

P = 128
D = 1024
KC = D // P
DEPTH = 2
HD = 64
GRID_W = 64
NA_KH = 8
NA_KW = 16
NB = 3
T = NB * P
BLOCKS = list(range(NB))
KEYS = T + P
HEADS = 8
TOPK = 16
PICKS = HEADS * TOPK
N_KEYS = 128
EXPERTS = N_KEYS * N_KEYS
ALPHA = (2 * DEPTH) ** 0.25
EPS = 1e-6
WT = 256
RING = 3
SLOTS = 4
GROUP = 4
BODY = 4
LOW = -3.0e38
ADA_T, IN_T, OUT_T, Q_T = 24, 7, 4, 8
PICKS_IT = BODY * GROUP
ITS = PICKS // PICKS_IT
assert ITS * NB == ADA_T
SH1, SC1, G1, SH2, SC2, G2 = (KC * i for i in range(6))
T_AQ, T_AKV, T_FX, T_NQ, T_NK, T_NV, T_PX = range(7)
JOBS = [(b, m, h) for b in range(NB) for m in range(2) for h in range(4)]
KEY_LO = [0, P, P]
KEY_HI = [P, KEYS, KEYS]


TURNS = 2 + NB + 1 + NB + 2 * NB + 2


def turn_at(l, what, b):
    return 1 + TURNS * l + {"ln1": 3 + b, "qk": 7 + b, "ln2": 10 + b, "back": 13 + b}[what]


INS = 5 * NB + 4


def cols_at(l):
    return ADA_T // RING + (1 + ADA_T) * l


def in_at(l, j, b):
    before = sum(2 if i in (T_NQ, T_NK) else NB for i in range(j))
    return INS * l + before + b + 1





def stream(b):
    return 0 if b == 0 else 1


class Steps:

    def __init__(self, eng):
        self.eng, self.taken, self.given = eng, {}, {}

    def take(self, sem, n=1, unit=1):
        k = self.taken[sem.name] = self.taken.get(sem.name, 0) + n
        self.eng.wait_ge(sem, k * unit)

    def free(self, sem, depth):
        k = self.taken[sem.name] = self.taken.get(sem.name, 0) + 1
        if k > depth:
            self.eng.wait_ge(sem, k - depth)

    def give(self, ins, sem):
        self.given[sem.name] = self.given.get(sem.name, 0) + 1
        ins.then_inc(sem, 1)

    def step(self, ins, sem):
        self.give(ins, sem)
        self.eng.wait_ge(sem, self.given[sem.name])


def program(nc, ins, outs):
    with ExitStack() as ctx:
        def sb(name, shape, dt=F32):
            return ctx.enter_context(nc.sbuf_tensor(name, shape, dt))

        def sem(name):
            return ctx.enter_context(nc.semaphore(name))

        ps = ctx.enter_context(nc.psum_tensor("ps", [P, 8, 512], F32))
        ps_turn = ps[:, 0:2, :].rearrange("p a n -> p (a n)")
        ps_proj = [ps[:, 2 + i, :] for i in range(2)]
        ps_sc = [ps[:, 4 + i, :] for i in range(2)]
        ps_pt = ps[:, 6, :]
        ps_o = ps[:, 7, :]
        ps_top = ps[:, 4:6, :].rearrange("p a n -> p (a n)")
        ps_y = [ps_turn, ps_top]
        ps_row = [ps_pt, ps_sc[0], ps_sc[1]]

        x = sb("x", [P, NB, D])
        hT = sb("hT", [P, KC, T])
        junk = sb("junk", [P, D])
        ada_tile = sb("ada_tile", [P, KC, WT])
        ada_row = [sb("ada_row", [2, WT])[:]] + [junk[0:2, 512 + i * WT:512 + (i + 1) * WT] for i in range(RING - 1)]
        h2 = sb("h2", [P, NB, D])
        mixT = sb("mixT", [P, KC, T])
        ring = sb("ring", [P, RING, KC, WT])
        ada_raw = sb("ada_raw", [P, 146])
        p_scale = ada_raw[:, 144:146]
        ada = sb("ada", [P, 6 * KC, 2])
        gate = sb("gate", [P, 2, D])
        ln_g = sb("ln_g", [P, D])
        ln_b = sb("ln_b", [P, D])
        stats = sb("stats", [P, NB, 2, 6])
        mv = sb("mv", [P, NB, 2])
        std = sb("std", [P, NB])
        rstd = sb("rstd", [P, NB])
        ident = sb("ident", [P, P])
        eps = sb("eps", [P, 1])
        zeros = sb("zeros", [P, P])
        crow = junk[0:2 * KC, 256:256 + P]
        silu_c = sb("silu_c", [P, 2, KC])
        dftL = sb("dftL", [P, 2, 2, 2 * P])
        dftP = sb("dftP", [P, 2, P])
        dftC = sb("dftC", [P, 2, P])
        poolL = sb("poolL", [P, 4, 2, 2 * P])
        poolP = sb("poolP", [P, 4, P])
        rope = sb("rope", [P, 2, 2, HD])
        na_mask = sb("na_mask", [P, 2, 2 * P])
        iota16 = sb("iota16", [P, TOPK])
        b_row = sb("b_row", [6 * KC + 2, P])
        qk_g = sb("qk_g", [P, 6, HD])
        na_b = sb("na_b", [P, 2, 4, 3 * P])
        wf = sb("wf", [P, 2, 2 * P])
        wp = sb("wp", [P, 2, HD])
        cache_k = sb("cache_k", [P, 3 * P])
        k12 = sb("k12", [P, 2, P])
        k12T = sb("k12T", [P, 2, P])
        qk = sb("qk", [P, NB, 6, HD])
        av = sb("av", [P, 4, P])
        nv = sb("nv", [P, 4, 2 * P])
        nk_out = junk[:, 0:2 * P]
        aqT = sb("aqT", [P, 2, T])
        akT = sb("akT", [P, KEYS])
        nqT = sb("nqT", [P, 2, T])
        nkT = sb("nkT", [P, 2, KEYS])
        ss = sb("ss", [P, NB, 6])
        ss2 = sb("ss2", [P, NB, 6])
        room = sb("room", [P, 2 * SLOTS * D])
        at = [0]

        def part(shape):
            n = 1
            for s in shape:
                n *= s
            v = room[:, at[0]:at[0] + n]
            at[0] += n
            assert at[0] <= 2 * SLOTS * D
            return v

        fx = part([NB, 2 * P]).rearrange("p (b n) -> p b n", b=NB)
        px = part([NB, 2 * P]).rearrange("p (b n) -> p b n", b=NB)
        dT = part([2, 2, T]).rearrange("p (c m n) -> p c m n", c=2, m=2)
        yT = part([2, T]).rearrange("p (c n) -> p c n", c=2)
        poolT = part([2, T]).rearrange("p (c n) -> p c n", c=2)
        mean_sq = at[0]
        prob = part([2, 3 * P]).rearrange("p (s n) -> p s n", s=2)
        probT = part([2, 3 * P]).rearrange("p (s n) -> p s n", s=2)
        rot = part([6, HD]).rearrange("p (h d) -> p h d", h=6)
        at[0] = mean_sq
        sq = part([NB, 6, HD]).rearrange("p (b h d) -> p b h d", b=NB, h=6)
        at[0] = 0
        xhat = part([NB, D]).rearrange("p (b n) -> p b n", b=NB)
        mixed = part([D])
        at[0] = 0
        u_rows = part([SLOTS, D]).rearrange("p (s n) -> p s n", s=SLOTS)
        v_rows = part([SLOTS, D]).rearrange("p (s n) -> p s n", s=SLOTS)

        nmax = sb("nmax", [P, 2])
        psums = sb("psums", [P, 2])
        pinv = sb("pinv", [P, 2])
        qT = [nqT, nkT[:, :, 0:T]]
        best = sb("best", [P, NB, 2, HEADS, TOPK])
        best_i = sb("best_i", [P, NB, 2, HEADS, TOPK], U32)
        n_cand = HEADS * TOPK * TOPK
        mix_flat, h_flat = (t[:].rearrange("p k n -> p (k n)") for t in (mixT, hT))
        cand = mix_flat[:, 0:n_cand].rearrange("p (h n) -> p h n", h=HEADS)
        scr = mix_flat[:, n_cand:n_cand + NB * 2 * N_KEYS].rearrange("p (i n) -> p i n", i=NB * 2)
        product = h_flat[:, 0:D]
        found = mix_flat[:, n_cand + 768:n_cand + 1024].rearrange("p (a h k) -> p a h k", a=2, h=HEADS)

        def choosing(flat):
            four = [flat[:, n_cand + i * PICKS:n_cand + (i + 2) * PICKS] for i in (1, 3, 5)]
            four[0] = four[0].bitcast(U32)
            return (flat[:, 0:n_cand].rearrange("p (h n) -> p h n", h=HEADS),
                    flat[:, n_cand:n_cand + PICKS].bitcast(U32).rearrange("p (h k) -> p h k", h=HEADS),
                    *(t.rearrange("p (a h k) -> p a h k", a=2, h=HEADS) for t in four))

        chooser = [choosing(room[:, 0:3 * D])] + [choosing(h_flat)] * (NB - 1)
        top = sb("top", [P, HEADS, TOPK])
        idx_f = mix_flat[:, 0:PICKS]
        idx = sb("idx", [P, 2, PICKS], U32)
        cur = sb("cur", [P, BODY, GROUP], U32)
        gsum = sb("gsum", [P, HEADS])
        gw = sb("gw", [P, 2, HEADS, TOPK])
        dots = sb("dots", [P, GROUP])
        gelu = sb("gelu", [P, GROUP])
        weight = sb("weight", [P, GROUP])
        diag = sb("diag", [P, SLOTS, P])

        w_landed = [sem(f"w_landed{i}") for i in range(RING)]
        w_free = sem("w_free")
        ada_tile_in = sem("ada_tile_in")
        row_done = sem("row_done")
        row_copied = sem("row_copied")
        col_done = sem("col_done")
        col_free = sem("col_free")
        consts_in = sem("consts_in")
        small_in = sem("small_in")
        small_used = sem("small_used")
        ln1_in = sem("ln1_in")
        ln2_in = sem("ln2_in")
        ln1_used = sem("ln1_used")
        ln2_used = sem("ln2_used")
        pool_ready = sem("pool_ready")
        turn_ready = sem("turn_ready")
        turn_free = sem("turn_free")
        proj_ready = sem("proj_ready")
        proj_free = sem("proj_free")
        ada_ready = sem("ada_ready")
        qk_ready = sem("qk_ready")
        gate_ready = sem("gate_ready")
        gate_used = sem("gate_used")
        dve_step = sem("dve_step")
        var_ready = sem("var_ready")
        std_ready = sem("std_ready")
        xhat_ready = sem("xhat_ready")
        hT_ready = sem("hT_ready")
        h2_ready = sem("h2_ready")
        in_ready = sem("in_ready")
        ss_ready = sem("ss_ready")
        srt_ready = sem("srt_ready")
        k_out_ready = sem("k_out_ready")
        k_out_done = sem("k_out_done")
        att_in_ready = sem("att_in_ready")
        nk_out_ready = sem("nk_out_ready")
        bias_ready = sem("bias_ready")
        side_ready = sem("side_ready")
        mix_side_ready = sem("mix_side_ready")
        s_ready = sem("s_ready")
        s_free = sem("s_free")
        nmax_ready = sem("nmax_ready")
        exp_ready = sem("exp_ready")
        prob_ready = sem("prob_ready")
        pt_ready = sem("pt_ready")
        probT_ready = sem("probT_ready")
        o_ready = sem("o_ready")
        o_free = sem("o_free")
        mo_ready = sem("mo_ready")
        mo_free = sem("mo_free")
        qT_ready = sem("qT_ready")
        top_ready = sem("top_ready")
        top_free = sem("top_free")
        gexp_in = sem("gexp_in")
        gexp_out = sem("gexp_out")
        idx_ready = sem("idx_ready")
        cur_ready = sem("cur_ready")
        pool_pace = sem("pool_pace")
        u_landed = [sem(f"u_landed{i}") for i in range(SLOTS)]
        v_landed = [sem(f"v_landed{i}") for i in range(SLOTS)]
        u_free = sem("u_free")
        v_free = sem("v_free")
        gelu_ready = sem("gelu_ready")
        weight_ready = sem("weight_ready")
        diag_ready = sem("diag_ready")
        y_cleared = sem("y_cleared")
        y_free = sem("y_free")
        x_ready = sem("x_ready")
        out_done = sem("out_done")

        w_view = [w.rearrange("l (k p) n -> l p k n", p=P)
                  for w in (ins["w_ada"], ins["w_in"], ins["w_out"], ins["peer_wq"])]
        table_u = ins["peer_u"].rearrange("l e d -> (l e) d")
        table_v = ins["peer_v"].rearrange("l e d -> (l e) d")

        block = ctx.enter_context(nc.Block())

        @block.sync
        def _(sp):
            sp.sem_inc(w_free, RING)
            with sp.Fori(0, ADA_T // RING) as i:
                for s in range(RING):
                    sp.wait_ge(w_free, i * RING + s + 1)
                    sp.dma_start(ring[:, s], w_view[0][0][:, :, bass.ds((i * RING + s) * WT, WT)]).then_inc(w_landed[s], 16)
            n = ADA_T
            for l in range(DEPTH):
                if l > 0:
                    with sp.Fori(0, ADA_T) as i:
                        sp.wait_ge(row_done, ADA_T * l + i)
                        sp.dma_start(ada_tile[:], w_view[0][l][:, :, bass.ds(i * WT, WT)]).then_inc(ada_tile_in, 16)
                for w, tiles in zip(w_view[1:], (IN_T, OUT_T, Q_T)):
                    for j in range(tiles):
                        sp.wait_ge(w_free, n + 1)
                        sp.dma_start(ring[:, n % RING], w[l][:, :, j * WT:(j + 1) * WT]).then_inc(w_landed[n % RING], 16)
                        n += 1

        @block.gpsimd
        def _(pool):
            st = Steps(pool)
            nc.gpsimd.memset(zeros[:], 0.0)
            nc.gpsimd.memset(eps[:], EPS)
            st.give(nc.gpsimd.iota(iota16[:], [[1, TOPK]], base=0, channel_multiplier=0,
                                   allow_small_or_imprecise_dtypes=True), pool_ready)
            pool.sem_inc(u_free, SLOTS)
            pool.sem_inc(v_free, SLOTS)
            for l in range(DEPTH):
                st.take(small_in, 1, 16 * 35)
                for qb in range(2):
                    for h in range(4):
                        ins_ = nc.gpsimd.tensor_tensor(na_b[:, qb, h, 0:2 * P], na_b[:, qb, h, 0:2 * P],
                                                       na_mask[:, qb, :], ALU.add)
                ins_ = nc.gpsimd.memset(na_b[:, :, :, 2 * P:3 * P], 0.0)
                st.give(ins_, bias_ready)
                for b in range(NB):
                    step = l * NB + b
                    st.take(idx_ready)
                    rows0 = step * PICKS // SLOTS

                    def copy_cur(base, g):
                        ins_ = nc.gpsimd.tensor_copy(cur[:, g % BODY, :], idx[:, step % 2, bass.ds(base * BODY * GROUP + g * GROUP, GROUP)]
                                                     if not isinstance(base, int) else
                                                     idx[:, step % 2, (base * BODY + g) * GROUP:(base * BODY + g + 1) * GROUP])
                        ins_.then_inc(cur_ready, 1)
                        pool.wait_ge(cur_ready, step * (PICKS // GROUP) + base * BODY + g + 1)
                        pool.sem_inc(pool_pace, 1)

                    def gather_u(base, g, m):
                        pool.wait_ge(u_free, step * PICKS + base * (BODY * GROUP) + g * GROUP + m + 1)
                        pool.sem_inc(pool_pace, 1)
                        nc.gpsimd.indirect_dma_start(u_rows[:, m, :], None, table_u,
                                                     bass.IndirectOffsetOnAxis(cur[:, g % BODY, m:m + 1], 0)).then_inc(u_landed[m], 16)

                    def gather_v(base, g, m):
                        pool.wait_ge(v_free, step * PICKS + base * (BODY * GROUP) + g * GROUP + m + 1)
                        pool.sem_inc(pool_pace, 1)
                        nc.gpsimd.indirect_dma_start(v_rows[:, m, :], None, table_v,
                                                     bass.IndirectOffsetOnAxis(cur[:, g % BODY, m:m + 1], 0)).then_inc(v_landed[m], 16)

                    def body(base, last):
                        for g in range(BODY):
                            ahead = not (last and g == BODY - 1)
                            if ahead:
                                copy_cur(base, g + 1)
                            for m in range(GROUP):
                                if ahead:
                                    gather_u(base, g + 1, m)
                                gather_v(base, g, m)

                    copy_cur(0, 0)
                    for m in range(GROUP):
                        gather_u(0, 0, m)
                    with pool.Fori(0, PICKS // (BODY * GROUP) - 1) as i:
                        body(i, False)
                    body(PICKS // (BODY * GROUP) - 1, True)

        @block.scalar
        def _(act):
            st = Steps(act)

            def load(dst, src, s):
                act.dma_start(dst, src).then_inc(s, 16)

            def load_small(l):
                load(b_row[0:6 * KC, :], ins["b_ada"][l].rearrange("(k p) -> k p", p=P), small_in)
                load(cache_k[:, 0:P], ins["cache_attn_k"][0, l].rearrange("t h d -> t (h d)"), small_in)
                load(cache_k[:, P:3 * P], ins["cache_na_k"][0, l].rearrange("t h d -> t (h d)"), small_in)
                load(av[:, 3, :], ins["cache_attn_v"][0, l].rearrange("t h d -> t (h d)"), small_in)
                load(nv[:, 3, :], ins["cache_na_v"][0, l].rearrange("t h d -> t (h d)"), small_in)
                for h in range(6):
                    g = ins["q_norm_g" if h < 4 else "k_norm_g"][l:l + 1, :]
                    load(qk_g[:, h, :], g.to_broadcast([P, HD]), small_in)
                load(wf[:], ins["w_fourier"][l].rearrange("(c p) n -> p c n", p=P), small_in)
                for g in range(4):
                    load(wp[64 * (g % 2):64 * (g % 2) + 64, g // 2, :], ins["w_pool"][l, g], small_in)
                load(b_row[6 * KC:6 * KC + 2, :], ins["pool_scale"][l].rearrange("(c p) -> c p", p=P), small_in)
                load(k12[:, 0, :], ins["peer_k1"][l], small_in)
                load(k12[:, 1, :], ins["peer_k2"][l], small_in)
                for r in range(4):
                    for h in range(4):
                        load(na_b[64 * (r % 2):64 * (r % 2) + 64, r // 2, h, 0:2 * P].rearrange("p (a b) -> p a b", a=4),
                             ins["na_bias_slid"][l, h, :, NA_KH - 1 - r:NA_KH + 3 - r, :], small_in)

            def load_ln(l, which, s):
                load(ln_g[:], ins[f"ln{which}_g"][l:l + 1, :].to_broadcast([P, D]), s)
                load(ln_b[:], ins[f"ln{which}_b"][l:l + 1, :].to_broadcast([P, D]), s)

            load(ident[:], ins["const_ident"], consts_in)
            load(crow[0:KC, :], ins["c_ctx"].rearrange("(k p) -> k p", p=P), consts_in)
            load(crow[KC:2 * KC, :], ins["c"][0].rearrange("(k p) -> k p", p=P), consts_in)
            load(x[:, 0, :], ins["x_prompt"][0], consts_in)
            load(x[:, 1:3, :], ins["x_sample"][0].rearrange("(b p) d -> p b d", p=P), consts_in)
            for t, name in ((dftL, "const_dft_latent"), (dftP, "const_dft_prompt"), (dftC, "const_dft_channel"),
                            (poolL, "const_pool_latent"), (poolP, "const_pool_prompt"), (rope, "const_rope"),
                            (na_mask, "const_na_mask")):
                load(t[:], ins[name], consts_in)
            load_small(0)
            load_ln(0, 1, ln1_in)
            act.wait_ge(consts_in, 16 * 12)
            act.wait_ge(pool_ready, 1)

            act.sem_inc(col_free, 1)
            st.take(turn_ready)
            st.step(nc.scalar.activation(silu_c[:], ps_turn[:, 0:2 * KC].rearrange("p (s k) -> p s k", s=2),
                                         ACT.Silu), turn_free)

            def root(given, out, in_, scale, done):
                st.take(given)
                st.give(nc.scalar.activation(out, in_, ACT.Sqrt, bias=eps[:], scale=scale), done)

            def root_all():
                root(var_ready, std[:], mv[:, :, 1], 1.0, std_ready)

            def copy_row(n, s):
                act.wait_ge(row_done, n + 1)
                nc.scalar.copy(ada_row[s], ps_row[s][0:2, 0:WT]).then_inc(row_copied, 1)

            def copy_col(n, dst, w):
                act.wait_ge(col_done, n + 1)
                nc.scalar.copy(dst, ps_o[:, 0:w]).then_inc(col_free, 1)

            def modulate(b, sh, sc):
                st.take(turn_ready)
                for k in range(KC):
                    ins_ = nc.scalar.activation(hT[:, k, b * P:(b + 1) * P], ps_turn[:, k * P:(k + 1) * P], ACT.Identity,
                                                bias=ada[:, sh + k, stream(b):stream(b) + 1],
                                                scale=ada[:, sc + k, stream(b):stream(b) + 1])
                st.step(ins_, turn_free)
                act.sem_inc(hT_ready, 1)

            def gates():
                for s in range(2):
                    st.take(turn_ready)
                    ins_ = nc.scalar.copy(gate[:, s, :], ps_turn)
                    st.step(ins_, turn_free)
                act.sem_inc(gate_ready, 1)

            for l in range(DEPTH):
                if l == 0:
                    with act.Fori(0, ADA_T // RING) as i:
                        for s in range(RING):
                            copy_row(i * RING + s, s)
                        copy_col(i, ada_raw[:, bass.ds(i * 4 * RING, 4 * RING)], 4 * RING)
                copy_col(cols_at(l), ada_raw[:, 96:146], 50)
                st.take(ada_ready)
                if l > 0:
                    act.wait_ge(gate_used, l * 2)
                gates()
                root_all()
                for b in range(NB):
                    modulate(b, SH1, SC1)

                def evacuate(*pairs, scale=1.0):
                    st.take(proj_ready)
                    src = ps_proj[st.taken["proj_ready"] % 2 ^ 1]
                    for dst, lo, hi in pairs:
                        part_ = src[:, lo:hi]
                        if len(dst.shape) == 4:
                            part_ = part_.rearrange("p (k g d) -> p k g d", k=2, g=2)
                        ins_ = nc.scalar.activation(dst, part_, ACT.Copy, scale=scale)
                    st.step(ins_, proj_free)
                    act.sem_inc(in_ready, 1)

                if l > 0:
                    act.wait_ge(out_done, 32 * l)
                for j in range(IN_T):
                    if j in (T_NQ, T_NK):
                        for c in range(2):
                            evacuate(((nqT if j == T_NQ else nkT)[:, c, 0:T], 0, T), scale=0.125 if j == T_NQ else 1.0)
                        continue
                    for b in range(NB):
                        if j == T_AQ:
                            evacuate((qk[:, b, 0:4, :].rearrange("p (g k) d -> p k g d", g=2), 0, 256))
                        elif j == T_AKV:
                            evacuate((qk[:, b, 4:6, :].rearrange("p h d -> p (h d)"), 0, 128), (av[:, b, :], 128, 256))
                        else:
                            evacuate(({T_FX: fx, T_NV: nv, T_PX: px}[j][:, b, :], 0, 256))
                    if j == T_FX:
                        root(ss_ready, ss2[:], ss[:], 1.0 / HD, srt_ready)
                act.dma_start(outs[3][0, l].rearrange("t h d -> t (h d)"), av[:, 0, :]).then_inc(out_done, 16)
                act.dma_start(outs[5][0, l].rearrange("t h d -> t (h d)"), nv[:, 0, :]).then_inc(out_done, 16)

                st.take(turn_ready)
                nc.scalar.copy(akT[:, T:KEYS], ps_turn[:, 0:P])
                nc.scalar.copy(nkT[:, :, T:KEYS], ps_turn[:, P:3 * P].rearrange("p (c n) -> p c n", c=2))
                nc.scalar.copy(k12T[:], ps_turn[:, 512:512 + 2 * P].rearrange("p (c n) -> p c n", c=2))
                if l > 0:
                    act.wait_ge(k_out_done, 32 * l)
                st.step(nc.scalar.copy(nk_out, ps_turn[:, 768:1024]), turn_free)
                act.sem_inc(att_in_ready, 1)
                act.dma_start(outs[4][0, l].rearrange("t h d -> t (h d)"), nk_out).then_inc(k_out_done, 16)

                def side(dst, lo, hi, plo=0, phi=P, scale=1.0, final=False):
                    st.take(proj_ready)
                    src = ps_proj[st.taken["proj_ready"] % 2 ^ 1]
                    st.step(nc.scalar.activation(dst, src[plo:phi, lo:hi], ACT.Copy, scale=scale), proj_free)
                    act.sem_inc(mix_side_ready if final else side_ready, 1)

                for c in range(2):
                    for m in range(2):
                        side(dT[:, c, m, :], 0, T)
                for c in range(2):
                    side(yT[:, c, :], 0, T)
                for c in range(2):
                    side(poolT[:, c, :], 0, T)
                for c in range(2):
                    side(mixT[:, 2 + c, :], 0, T, final=True)
                for c in range(2):
                    side(mixT[:, 6 + c, :], 0, T, scale=p_scale[:, c:c + 1], final=True)

                act.wait_ge(k_out_ready, l + 1)
                act.dma_start(outs[2][0, l].rearrange("t h d -> t (h d)"),
                              qk[:, 0, 4:6, :].rearrange("p h d -> p (h d)")).then_inc(k_out_done, 16)
                for b in range(NB):
                    st.take(turn_ready)
                    nc.scalar.activation(aqT[:, :, b * P:(b + 1) * P], ps_turn[:, 0:2 * P].rearrange("p (c n) -> p c n", c=2),
                                         ACT.Copy, scale=0.125)
                    st.step(nc.scalar.copy(akT[:, b * P:(b + 1) * P], ps_turn[:, 2 * P:3 * P]), turn_free)
                    act.sem_inc(att_in_ready, 1)

                def copy_t(n):
                    b, m, h = JOBS[n]
                    w = KEY_HI[b] - KEY_LO[b]
                    st.take(pt_ready)
                    if n >= 2:
                        act.wait_ge(o_ready, l * len(JOBS) + n - 1)
                    st.step(nc.scalar.copy(probT[:, n % 2, 0:w], ps_pt[:, 0:w]), probT_ready)

                def exponent(n):
                    b, m, h = JOBS[n]
                    w = KEY_HI[b] - KEY_LO[b]
                    st.take(nmax_ready)
                    if n >= 2:
                        act.wait_ge(pt_ready, l * len(JOBS) + n - 1)
                    st.step(nc.scalar.activation(prob[:, n % 2, 0:w], ps_sc[n % 2][:, 0:w], ACT.Exp, bias=nmax[:, n % 2:n % 2 + 1],
                                                 accum_out=psums[:, n % 2:n % 2 + 1]), exp_ready)

                def head_out(n):
                    if n % 2:
                        b, m, h = JOBS[n]
                        act.wait_ge(o_ready, l * len(JOBS) + n + 1)
                        st.step(nc.scalar.copy(mixT[:, (4 if m else 0) + h // 2, b * P:(b + 1) * P], ps_o[:, 0:P]), o_free)

                for n in range(len(JOBS)):
                    exponent(n)
                    if n >= 1:
                        copy_t(n - 1)
                    if n >= 2:
                        head_out(n - 2)
                copy_t(len(JOBS) - 1)
                head_out(len(JOBS) - 2)
                head_out(len(JOBS) - 1)

                root_all()
                act.wait_ge(ln1_used, l + 1)
                load_ln(l, 2, ln2_in)
                root_all()
                for b in range(NB):
                    modulate(b, SH2, SC2)
                for j in range(Q_T):
                    for half in range(2):
                        st.take(proj_ready)
                        if j > 1:
                            act.wait_ge(top_ready, l * Q_T + j - 1)
                        st.step(nc.scalar.copy(qT[j % 2][:, half, :], ps_proj[st.taken["proj_ready"] % 2 ^ 1][:, 0:T]), proj_free)
                        act.sem_inc(qT_ready, 1)
                    if j < NB:
                        st.take(turn_ready)
                        st.step(nc.scalar.copy(h2[:, j, :], ps_turn), turn_free)
                        act.sem_inc(h2_ready, 1)
                    elif j == NB:
                        act.wait_ge(gate_used, 2 * l + 1)
                        gates()
                if l + 1 < DEPTH:
                    st.take(small_used)
                    load_small(l + 1)
                def weights_exp(turn):
                    st.take(gexp_in)
                    st.give(nc.scalar.activation(gw[:, turn % 2], gw[:, turn % 2], ACT.Exp), gexp_out)

                def finish(b):
                    root(var_ready, std[:, b:b + 1], mv[:, b, 1:2], 1.0, std_ready)
                    if l + 1 == DEPTH:
                        act.wait_ge(x_ready, l * NB + b + 1)
                        dst = outs[0][0] if b == 0 else outs[1][0, (b - 1) * P:b * P, :]
                        act.dma_start(dst, x[:, b, :]).then_inc(out_done, 16)

                act.wait_ge(k_out_done, 32 * (l + 1))
                weights_exp(l * NB)
                for b in range(NB):
                    step = l * NB + b

                    def iteration(i):
                        for g in range(BODY):
                            group(i, g)
                            if l + 1 < DEPTH and g == 0:
                                copy_row(ADA_T + b * ITS + i, 0)
                            if l + 1 < DEPTH and g == 2:
                                dst = (bass.ds(i * 4 + b * ITS * 4, 4) if not isinstance(i, int) else
                                       slice((b * ITS + i) * 4, (b * ITS + i + 1) * 4))
                                copy_col(ADA_T // RING + 1 + b * ITS + i, ada_raw[:, dst], 4)

                    def group(base, g):
                        first = step * PICKS + base * (BODY * GROUP) + g * GROUP
                        turn = step * (PICKS // GROUP) + base * BODY + g
                        act.wait_ge(u_free, first + GROUP + SLOTS)
                        nc.scalar.activation(gelu[:], dots[:], ACT.Gelu).then_inc(gelu_ready, 1)
                        act.wait_ge(weight_ready, turn + 1)
                        for m in range(GROUP):
                            act.wait_ge(v_free, first + m + 1)
                            nc.scalar.activation(diag[:, m, :], ident[:], ACT.Copy,
                                                 scale=weight[:, m:m + 1]).then_inc(diag_ready, 1)

                    iteration(0)
                    if b > 0:
                        finish(b - 1)
                    with act.Fori(1, ITS) as i:
                        iteration(i)
                    if b + 1 < NB:
                        weights_exp(step + 1)
                finish(NB - 1)
                if l + 1 < DEPTH:
                    act.wait_ge(ln2_used, l + 1)
                    load_ln(l + 1, 1, ln1_in)
            act.wait_ge(out_done, 16 * (2 * DEPTH + NB))
            act.wait_ge(k_out_done, 32 * DEPTH)

        @block.vector
        def _(dve):
            st = Steps(dve)
            V = nc.vector

            def step(ins_):
                st.step(ins_, dve_step)

            dve.wait_ge(consts_in, 16 * 12)
            dve.wait_ge(pool_ready, 1)

            def norm_stats(bs):
                for b in bs:
                    for half in range(2):
                        ins_ = V.bn_stats(stats[:, b, half, :], x[:, b, half * 512:(half + 1) * 512])
                step(ins_)
                for b in bs:
                    ins_ = V.bn_aggr(mv[:, b, :], stats[:, b].rearrange("p a b -> p (a b)"))
                st.step(ins_, var_ready)
                st.take(std_ready)
                step(V.reciprocal(rstd[:, bs[0]:bs[-1] + 1], std[:, bs[0]:bs[-1] + 1]))

            def normalize(dst, b):
                return V.tensor_scalar(dst, x[:, b, :], mv[:, b, 0:1], rstd[:, b:b + 1], ALU.subtract, ALU.mult)

            def post_norm(bs, final):
                norm_stats(bs)
                for b in bs:
                    ins_ = normalize(x[:, b, :], b)
                step(ins_)
                for b in bs:
                    ins_ = V.tensor_tensor(x[:, b, :], x[:, b, :], ln_g[:], ALU.mult)
                step(ins_)
                for b in bs:
                    ins_ = V.tensor_tensor(x[:, b, :], x[:, b, :], ln_b[:], ALU.add)
                st.step(ins_, final)

            def normalized():
                norm_stats(BLOCKS)
                for b in BLOCKS:
                    st.step(normalize(xhat[:, b, :], b), xhat_ready)

            for l in range(DEPTH):
                st.take(small_in, 1, 16 * 35)
                dve.wait_ge(col_free, cols_at(l) + 2)
                step(V.tensor_tensor(ada[:], ada_raw[:, 0:96].rearrange("p (c s) -> p c s", s=2),
                                     ada_raw[:, 96:144].unsqueeze(2).to_broadcast([P, 6 * KC, 2]), ALU.add))
                V.tensor_scalar(ada[:, SC1:SC1 + KC, :], ada[:, SC1:SC1 + KC, :], 1.0, None, ALU.add)
                st.step(V.tensor_scalar(ada[:, SC2:SC2 + KC, :], ada[:, SC2:SC2 + KC, :], 1.0, None, ALU.add), ada_ready)

                normalized()

                dve.wait_ge(in_ready, in_at(l, T_AKV, NB - 1))
                step(V.tensor_tensor(sq, qk[:], qk[:], ALU.mult))
                st.step(V.tensor_reduce(ss[:], sq, AX_X, ALU.add), ss_ready)
                st.take(srt_ready)
                step(V.reciprocal(ss[:], ss2[:]))
                step(V.tensor_tensor(qk[:], qk[:], ss[:].unsqueeze(3).to_broadcast([P, NB, 6, HD]), ALU.mult))
                st.step(V.tensor_tensor(qk[:], qk[:], qk_g[:].unsqueeze(1).to_broadcast([P, NB, 6, HD]), ALU.mult), k_out_ready)
                for b in range(1, NB):
                    cos = rope[:, b - 1, 0, :].unsqueeze(1).to_broadcast([P, 6, HD])
                    sin = rope[:, b - 1, 1, :].rearrange("p (e d) -> p e d", e=4)
                    r5 = rot.rearrange("p h (e d) -> p h e d", e=4)
                    s5 = qk[:, b].rearrange("p h (e d) -> p h e d", e=4)
                    for e in range(4):
                        ins_ = V.tensor_tensor(r5[:, :, e, :], s5[:, :, e ^ 1, :],
                                               sin[:, e, :].unsqueeze(1).to_broadcast([P, 6, 16]), ALU.mult)
                    step(ins_)
                    step(V.tensor_tensor(qk[:, b], qk[:, b], cos, ALU.mult))
                    st.step(V.tensor_tensor(qk[:, b], qk[:, b], rot, ALU.add), qk_ready)

                J = len(JOBS)

                def maximum(n):
                    b, m, h = JOBS[n]
                    w = KEY_HI[b] - KEY_LO[b]
                    st.take(s_ready)
                    src = ps_sc[n % 2][:, 0:w]
                    st.step(V.tensor_reduce(nmax[:, n % 2:n % 2 + 1], src, AX_X, ALU.max, negate=True), nmax_ready)

                def divide(n):
                    b, m, h = JOBS[n]
                    w = KEY_HI[b] - KEY_LO[b]
                    st.take(exp_ready)
                    step(V.reciprocal(pinv[:, n % 2:n % 2 + 1], psums[:, n % 2:n % 2 + 1]))
                    st.step(V.tensor_scalar(prob[:, n % 2, 0:w], prob[:, n % 2, 0:w], pinv[:, n % 2:n % 2 + 1], None,
                                            ALU.mult), prob_ready)

                maximum(0)
                for n in range(J):
                    if n + 1 < J:
                        maximum(n + 1)
                    divide(n)

                st.take(gate_ready)
                for j in range(OUT_T):
                    for b in range(NB):
                        c = slice(j * WT, (j + 1) * WT)
                        st.take(mo_ready)
                        st.step(V.tensor_tensor(mixed[:, c], ps_sc[(j * NB + b) % 2][:, 0:WT], gate[:, stream(b), c], ALU.mult), mo_free)
                        step(V.scalar_tensor_tensor(x[:, b, c], x[:, b, c], ALPHA, mixed[:, c], ALU.mult, ALU.add))
                dve.sem_inc(gate_used, 1)
                st.take(ln1_in, 2, 16)
                post_norm(BLOCKS, dve_step)
                dve.sem_inc(ln1_used, 1)
                normalized()

                def choose(b, h):
                    cand2, pos = chooser[b][0:2]
                    step(V.tensor_tensor(cand[:, h, :].rearrange("p (i j) -> p i j", i=TOPK),
                                         best[:, b, 0, h].unsqueeze(2).to_broadcast([P, TOPK, TOPK]),
                                         best[:, b, 1, h].unsqueeze(1).to_broadcast([P, TOPK, TOPK]), ALU.add))
                    step(V.max(top[:, h, 0:8], cand[:, h, :]))
                    V.max_index(pos[:, h, 0:8], top[:, h, 0:8], cand[:, h, :])
                    step(V.match_replace(cand2[:, h, :], top[:, h, 0:8], cand[:, h, :], LOW))
                    step(V.max(top[:, h, 8:16], cand2[:, h, :]))
                    step(V.max_index(pos[:, h, 8:16], top[:, h, 8:16], cand2[:, h, :]))

                def pieces_of(b):
                    cand2, pos, pos_ij, pos_f, best_f = chooser[b]
                    turn = l * NB + b
                    full = [P, HEADS, TOPK, TOPK]
                    c4 = cand.rearrange("p h (k i) -> p h k i", k=TOPK)
                    c5 = cand2.rearrange("p h (k i) -> p h k i", k=TOPK)

                    def split():
                        st.step(V.tensor_tensor(gw[:, turn % 2], top[:], top[:, :, 0:1].to_broadcast([P, HEADS, TOPK]),
                                                ALU.subtract), gexp_in)
                        V.tensor_scalar(pos_ij[:, 0], pos, 4, None, ALU.logical_shift_right)
                        step(V.tensor_scalar(pos_ij[:, 1], pos, 15, None, ALU.bitwise_and))
                        V.tensor_copy(pos_f, pos_ij)
                        step(V.tensor_copy(best_f, best_i[:, b]))

                    def equal(half):
                        step(V.tensor_tensor(c4, pos_f[:, half].unsqueeze(3).to_broadcast(full),
                                             iota16[:].unsqueeze(1).unsqueeze(1).to_broadcast(full), ALU.is_equal))

                    def masked(half):
                        step(V.tensor_tensor(c5, c4, best_f[:, half].unsqueeze(2).to_broadcast(full), ALU.mult))

                    def summed(half):
                        step(V.tensor_reduce(found[:, half], c5, AX_X, ALU.add))

                    def index():
                        step(V.tensor_scalar(idx_f.rearrange("p (h k) -> p h k", h=HEADS), found[:, 0], float(N_KEYS),
                                             float(l * EXPERTS), ALU.mult, ALU.add))
                        st.step(V.tensor_tensor(idx[:, turn % 2].rearrange("p (h k) -> p h k", h=HEADS),
                                                idx_f.rearrange("p (h k) -> p h k", h=HEADS), found[:, 1], ALU.add), idx_ready)

                    return [lambda h=h: choose(b, h) for h in range(HEADS)] + [split] + [
                        lambda f=f, half=half: f(half) for half in range(2) for f in (equal, masked, summed)] + [index]

                for j in range(Q_T):
                    st.take(top_ready)
                    pick = [(b, half) for b in range(NB) for half in range(2)]
                    src = [ps_top[:, i * P:(i + 1) * P] for i in range(6)]
                    for i, (b, half) in enumerate(pick):
                        ins_ = V.max(best[:, b, half, j, 0:8], src[i])
                    step(ins_)
                    for i, (b, half) in enumerate(pick):
                        V.max_index(best_i[:, b, half, j, 0:8], best[:, b, half, j, 0:8], src[i])
                        ins_ = V.match_replace(scr[:, i, :], best[:, b, half, j, 0:8], src[i], LOW)
                    st.step(ins_, top_free)
                    for i, (b, half) in enumerate(pick):
                        ins_ = V.max(best[:, b, half, j, 8:16], scr[:, i, :])
                    step(ins_)
                    for i, (b, half) in enumerate(pick):
                        ins_ = V.max_index(best_i[:, b, half, j, 8:16], best[:, b, half, j, 8:16], scr[:, i, :])
                    step(ins_)

                    choose(0, j)

                st.take(gate_ready)
                st.take(ln2_in, 2, 16)
                for piece in pieces_of(0)[HEADS:]:
                    piece()
                st.take(h2_ready, NB)
                for b in range(NB):
                    turn = l * NB + b
                    st.take(gexp_out)
                    step(V.tensor_reduce(gsum[:], gw[:, turn % 2], AX_X, ALU.add))
                    step(V.reciprocal(gsum[:], gsum[:]))
                    step(V.tensor_tensor(gw[:, turn % 2], gw[:, turn % 2], gsum[:].unsqueeze(2).to_broadcast([P, HEADS, TOPK]), ALU.mult))

                    gflat = gw[:, turn % 2].rearrange("p h k -> p (h k)")

                    def group(base, g):
                        first = turn * PICKS + base * (BODY * GROUP) + g * GROUP
                        for m in range(GROUP):
                            row = turn * (PICKS // SLOTS) + base * BODY + g
                            dve.wait_ge(u_landed[m], (row + 1) * 16)
                            dve.wait_ge(u_free, first + m + SLOTS)
                            V.tensor_tensor_reduce(out=junk[:], in0=u_rows[:, m, :], in1=h2[:, b, :], scale=1.0, scalar=0.0,
                                                   op0=ALU.mult, op1=ALU.add, accum_out=dots[:, m:m + 1]).then_inc(u_free, 1)
                        dve.wait_ge(gelu_ready, turn * (PICKS // GROUP) + base * BODY + g + 1)
                        at_ = (bass.ds(base * (BODY * GROUP) + g * GROUP, GROUP) if not isinstance(base, int) else
                               slice((base * BODY + g) * GROUP, (base * BODY + g + 1) * GROUP))
                        V.tensor_tensor(weight[:], gelu[:], gflat[:, at_], ALU.mult).then_inc(weight_ready, 1)
                        dve.wait_ge(weight_ready, turn * (PICKS // GROUP) + base * BODY + g + 1)

                    def update(b):
                        last = l * NB + b
                        dve.wait_ge(v_free, (last + 1) * PICKS + SLOTS)
                        st.step(V.tensor_tensor(product, ps_y[last % 2], gate[:, stream(b), :], ALU.mult), y_free)
                        step(V.scalar_tensor_tensor(x[:, b, :], x[:, b, :], ALPHA, product, ALU.mult, ALU.add))
                        post_norm([b], x_ready)

                    for g in range(BODY):
                        group(0, g)
                    if b > 0:
                        update(b - 1)
                    tail = 3 if b + 1 < NB else 0
                    with dve.Fori(1, ITS - tail) as i:
                        for g in range(BODY):
                            group(i, g)
                    pieces = pieces_of(b + 1) if tail else []
                    for i in range(ITS - tail, ITS):
                        for g in range(BODY):
                            group(i, g)
                            for piece in pieces[:2]:
                                piece()
                            pieces = pieces[2:]
                    assert not pieces
                update(NB - 1)
                dve.sem_inc(gate_used, 1)
                dve.sem_inc(ln2_used, 1)

        @block.tensor
        def _(pe):
            st = Steps(pe)
            M = nc.tensor

            zero_by = dftL[:].rearrange("p m k n -> p (m k n)")
            tiles = [ADA_T]

            def weights():
                n = tiles[0]
                tiles[0] += 1
                pe.wait_ge(w_landed[n % RING], 16 * (n // RING + 1))
                return ring[:, n % RING]

            def rows(w, s):
                for k in range(KC):
                    ins_ = M.matmul(ps_row[s][0:2, 0:WT], silu_c[:, :, k], w[:, k, :], start=(k == 0), stop=(k == KC - 1))
                return ins_

            def cols(s):
                for m in range(2):
                    ins_ = M.matmul(ps_o[:, 4 * s + 2 * m:4 * s + 2 * m + 2], ada_row[s][:, m * P:(m + 1) * P], ident[0:2, 0:2],
                                    start=True, stop=True)
                return ins_

            projs = [0]

            def proj():
                st.free(proj_free, 2)
                projs[0] += 1
                return ps_proj[(projs[0] - 1) % 2]

            def turn_in():
                st.free(turn_free, 1)

            pe.wait_ge(consts_in, 16 * 12)
            pe.wait_ge(pool_ready, 1)
            turn_in()
            st.give(M.transpose(ps_turn[:, 0:2 * KC], crow, ident[0:2 * KC, 0:2 * KC]), turn_ready)
            pe.wait_ge(turn_free, 1)

            def transposes(b):
                for k in range(KC):
                    ins_ = M.transpose(ps_turn[:, k * P:(k + 1) * P], xhat[:, b, k * P:(k + 1) * P], ident[:])
                st.give(ins_, turn_ready)

            def gates(g):
                for s in range(2):
                    turn_in()
                    for k in range(KC):
                        ins_ = M.matmul(ps_turn[:, k * P:(k + 1) * P], ada[:, g + k, s:s + 1].to_broadcast([P, P]), ident[:],
                                        start=True, stop=True)
                    st.give(ins_, turn_ready)

            for l in range(DEPTH):
                J = len(JOBS)
                pe.wait_ge(small_in, 16 * 35 * (l + 1))
                if l == 0:
                    with pe.Fori(0, ADA_T // RING) as i:
                        for s in range(RING):
                            pe.wait_ge(w_landed[s], (i + 1) * 16)
                            rows(ring[:, s], s).then_inc(row_done, 1)
                        pe.wait_ge(col_free, i + 1)
                        for s in range(RING):
                            pe.wait_ge(row_copied, i * RING + s + 1)
                            pe.sem_inc(w_free, 1)
                            ins_ = cols(s)
                        ins_.then_inc(col_done, 1)
                pe.wait_ge(col_free, cols_at(l) + 1)
                M.transpose(ps_o[:, 0:50], b_row[:], ident[0:6 * KC + 2, 0:6 * KC + 2]).then_inc(col_done, 1)
                st.take(ada_ready)
                if l > 0:
                    pe.wait_ge(y_free, NB * l)
                gates(G1)
                for b in range(NB):
                    st.take(xhat_ready)
                    turn_in()
                    transposes(b)

                st.take(hT_ready, NB)
                for j in range(IN_T):
                    w = weights()
                    if j in (T_NQ, T_NK):
                        for c in range(2):
                            out = proj()
                            for k in range(KC):
                                ins_ = M.matmul(out[:, 0:T], w[:, k, c * P:(c + 1) * P], hT[:, k, :], start=(k == 0), stop=(k == KC - 1))
                            if c == 0:
                                st.give(ins_, proj_ready)
                    else:
                        for b in range(NB):
                            out = proj()
                            for k in range(KC):
                                ins_ = M.matmul(out[:, 0:WT], hT[:, k, b * P:(b + 1) * P], w[:, k, :], start=(k == 0), stop=(k == KC - 1))
                            if b < NB - 1:
                                st.give(ins_, proj_ready)
                    st.give(ins_, proj_ready)
                    pe.wait_ge(proj_ready, st.given["proj_ready"])
                    pe.sem_inc(w_free, 1)

                pe.wait_ge(in_ready, in_at(l, T_PX, NB - 1))
                turn_in()
                for c in range(3):
                    M.transpose(ps_turn[:, c * P:(c + 1) * P], cache_k[:, c * P:(c + 1) * P], ident[:])
                for c in range(2):
                    M.transpose(ps_turn[:, 512 + c * P:512 + (c + 1) * P], k12[:, c, :], ident[:])
                for c in range(2):
                    ins_ = M.transpose(ps_turn[:, 768 + c * P:768 + (c + 1) * P], nkT[:, c, 0:P], ident[:])
                st.give(ins_, turn_ready)

                for c in range(2):
                    for m in range(2):
                        out = proj()
                        cc = slice(c * P, (c + 1) * P)
                        M.matmul(out[:, 0:P], fx[:, 0, cc], dftP[:, m, :], start=True, stop=True)
                        for k in range(2):
                            ins_ = M.matmul(out[:, P:T], fx[:, 1 + k, cc], dftL[:, m, k, :], start=(k == 0), stop=(k == 1))
                        st.give(ins_, proj_ready)
                st.take(side_ready, 4)
                for c in range(2):
                    out = proj()
                    for m in range(2):
                        ins_ = M.matmul(out[:, 0:T], dftC[:, m, :], dT[:, c, m, :], start=(m == 0), stop=(m == 1))
                    st.give(ins_, proj_ready)
                for c in range(2):
                    out = proj()
                    for g in (2 * c, 2 * c + 1):
                        lo, cc = 64 * (g % 2), slice(g * HD, (g + 1) * HD)
                        M.matmul(out[lo:lo + 64, 0:P], px[:, 0, cc], poolP[:, g, :], start=True, stop=True)
                        for k in range(2):
                            ins_ = M.matmul(out[lo:lo + 64, P:T], px[:, 1 + k, cc], poolL[:, g, k, :], start=(k == 0), stop=(k == 1))
                    st.give(ins_, proj_ready)
                st.take(side_ready, 2)
                for c in range(2):
                    out = proj()
                    for k in range(2):
                        ins_ = M.matmul(out[:, 0:T], wf[:, k, c * P:(c + 1) * P], yT[:, k, :], start=(k == 0), stop=(k == 1))
                    st.give(ins_, proj_ready)
                st.take(side_ready, 2)
                for c in range(2):
                    out = proj()
                    for lo in (0, 64):
                        ins_ = M.matmul(out[lo:lo + 64, 0:T], wp[lo:lo + 64, c, :], poolT[lo:lo + 64, c, :], start=True, stop=True)
                    st.give(ins_, proj_ready)

                for b in range(NB):
                    if b == 0:
                        pe.wait_ge(k_out_ready, l + 1)
                    else:
                        st.take(qk_ready)
                    turn_in()
                    for g in range(2):
                        M.transpose(ps_turn[:, g * P:(g + 1) * P], qk[:, b, 2 * g:2 * g + 2, :].rearrange("p h d -> p (h d)"), ident[:])
                    st.give(M.transpose(ps_turn[:, 2 * P:3 * P], qk[:, b, 4:6, :].rearrange("p h d -> p (h d)"), ident[:]), turn_ready)

                pe.wait_ge(att_in_ready, (l + 1) * (1 + NB))
                st.take(bias_ready)

                def scores(n):
                    b, m, h = JOBS[n]
                    lo, hi = KEY_LO[b], KEY_HI[b]
                    q, keys = (nqT, nkT[:, h // 2, :]) if m else (aqT, akT)
                    r, c = (h % 2, h // 2) if m else (h // 2, h % 2)
                    if n >= 2:
                        pe.wait_ge(exp_ready, l * J + n - 1)
                    near = m and b
                    ins_ = M.matmul(ps_sc[n % 2][:, 0:hi - lo], q[64 * r:64 * r + 64, c, b * P:(b + 1) * P],
                                    keys[64 * r:64 * r + 64, lo:hi], start=True, stop=not near)
                    if near:
                        ins_ = M.matmul(ps_sc[n % 2][:, 0:hi - lo], ident[:], na_b[:, b - 1, h, :], start=False, stop=True)
                    st.give(ins_, s_ready)

                def turn_probs(n):
                    b, m, h = JOBS[n]
                    st.take(prob_ready)
                    if n >= 1:
                        pe.wait_ge(probT_ready, l * J + n)
                    for k in range((KEY_HI[b] - KEY_LO[b]) // P):
                        ins_ = M.transpose(ps_pt[:, k * P:(k + 1) * P], prob[:, n % 2, k * P:(k + 1) * P], ident[:])
                    st.give(ins_, pt_ready)

                def values(n):
                    b, m, h = JOBS[n]
                    st.take(probT_ready)
                    if n % 2 == 0:
                        st.free(o_free, 1)
                    nk = (KEY_HI[b] - KEY_LO[b]) // P
                    lo = 64 * (h % 2)
                    v = nv[:, :, h * HD:(h + 1) * HD] if m else av[:, :, (h // 2) * HD:(h // 2 + 1) * HD]
                    for k in range(nk):
                        ins_ = M.matmul(ps_o[lo:lo + 64, 0:P], v[:, KEY_LO[b] // P + k, :], probT[:, n % 2, k * P:(k + 1) * P],
                                        start=(k == 0), stop=(k == nk - 1))
                    st.give(ins_, o_ready)

                scores(0)
                for n in range(J):
                    if n + 1 < J:
                        scores(n + 1)
                    turn_probs(n)
                    if n >= 1:
                        values(n - 1)
                values(J - 1)

                st.take(mix_side_ready, 4)
                pe.wait_ge(o_free, (l + 1) * J // 2)
                for j in range(OUT_T):
                    w = weights()
                    for b in range(NB):
                        st.free(mo_free, 2)
                        for k in range(KC):
                            ins_ = M.matmul(ps_sc[(j * NB + b) % 2][:, 0:WT], mixT[:, k, b * P:(b + 1) * P], w[:, k, :],
                                            start=(k == 0), stop=(k == KC - 1))
                        st.give(ins_, mo_ready)
                    pe.wait_ge(mo_ready, st.given["mo_ready"])
                    pe.sem_inc(w_free, 1)
                for b in range(NB):
                    st.take(xhat_ready)
                    turn_in()
                    transposes(b)
                st.take(hT_ready, NB)

                def key_scores(j):
                    st.take(qT_ready, 2)
                    if j == 0:
                        pe.wait_ge(mo_free, (l + 1) * OUT_T * NB)
                    st.free(top_free, 1)
                    for b in range(NB):
                        for half in range(2):
                            i = b * 2 + half
                            ins_ = M.matmul(ps_top[:, i * P:(i + 1) * P], qT[j % 2][:, half, b * P:(b + 1) * P], k12T[:, half, :],
                                            start=True, stop=True)
                    st.give(ins_, top_ready)

                for j in range(Q_T):
                    w = weights()
                    for half in range(2):
                        out = proj()
                        for k in range(KC):
                            ins_ = M.matmul(out[:, 0:T], w[:, k, half * P:(half + 1) * P], hT[:, k, :], start=(k == 0), stop=(k == KC - 1))
                        st.give(ins_, proj_ready)
                    pe.wait_ge(proj_ready, st.given["proj_ready"])
                    pe.sem_inc(w_free, 1)
                    if j > 0:
                        key_scores(j - 1)
                    if j < NB:
                        turn_in()
                        for k in range(KC):
                            ins_ = M.transpose(ps_turn[:, k * P:(k + 1) * P], hT[:, k, j * P:(j + 1) * P], ident[:])
                        st.give(ins_, turn_ready)
                    elif j == NB:
                        gates(G2)
                key_scores(Q_T - 1)
                pe.wait_ge(top_ready, (l + 1) * Q_T)
                pe.sem_inc(small_used, 1)
                for b in range(NB):
                    turn = l * NB + b
                    y = ps_y[turn % 2]
                    if b == 0:
                        pe.wait_ge(turn_free, 1 + TURNS * (l + 1))
                        pe.wait_ge(top_free, Q_T * (l + 1))
                    if turn >= 2:
                        pe.wait_ge(y_free, turn - 1)
                    for half in range(2):
                        M.matmul(y[:, half * 512:(half + 1) * 512], zeros[:], zero_by[:, half * 512:(half + 1) * 512],
                                 start=True, stop=True, skip_group_check=True)

                    def group(base, g):
                        first = turn * PICKS + base * (BODY * GROUP) + g * GROUP
                        for m in range(GROUP):
                            pe.wait_ge(diag_ready, first + m + 1)
                            pe.wait_ge(v_landed[m], (turn * (PICKS // SLOTS) + base * BODY + g + 1) * 16)
                            for half in range(2):
                                ins_ = M.matmul(y[:, half * 512:(half + 1) * 512], diag[:, m, :],
                                                v_rows[:, m, half * 512:(half + 1) * 512], start=False, stop=True,
                                                skip_group_check=True)
                            ins_.then_inc(v_free, 1)

                    def next_map(i, g):
                        n = b * ITS + i
                        if g == 0:
                            pe.wait_ge(ada_tile_in, (n + 1) * 16)
                            rows(ada_tile, 0).then_inc(row_done, 1)
                        if g == 2:
                            pe.wait_ge(row_copied, n + ADA_T + 1)
                            pe.wait_ge(col_free, n + ADA_T // RING + 2)
                            cols(0).then_inc(col_done, 1)

                    with pe.Fori(0, ITS) as i:
                        for g in range(BODY):
                            group(i, g)
                            if l + 1 < DEPTH:
                                next_map(i, g)


_INS = ["x_prompt", "x_sample", "cache_attn_k", "cache_attn_v", "cache_na_k", "cache_na_v", "c", "c_ctx", "w_ada", "b_ada",
        "w_in", "q_norm_g", "k_norm_g", "w_fourier", "w_pool", "pool_scale", "w_out", "ln1_g", "ln1_b",
        "ln2_g", "ln2_b", "peer_wq", "peer_k1", "peer_k2", "peer_u", "peer_v"]
_OUTS = [(1, 128, 1024), (1, 256, 1024), (1, 2, 128, 2, 64), (1, 2, 128, 2, 64), (1, 2, 128, 4, 64), (1, 2, 128, 4, 64)]


def constants():
    import numpy as np

    def dft(n):
        a = 2 * np.pi * (np.outer(np.arange(n), np.arange(n)) % n) / n
        return np.cos(a), np.sin(a)

    out = {"const_ident": np.eye(P)}
    c, s = (t / np.sqrt(2 * P * HD) for t in dft(2 * P))
    out["const_dft_latent"] = np.stack([c, s]).reshape(2, 2, P, 2 * P).transpose(2, 0, 1, 3)
    c, s = (t / np.sqrt(P * HD) for t in dft(P))
    out["const_dft_prompt"] = np.stack([c, s]).transpose(1, 0, 2)
    c, s = dft(HD)
    out["const_dft_channel"] = np.stack([np.kron(np.eye(2), c), np.kron(np.eye(2), -s)]).transpose(1, 0, 2)

    def pool(n):
        m = np.zeros((4, n, n))
        for g, w in enumerate((2, 4, 8, 16)):
            for t in range(n):
                lo, hi = np.clip([t - w // 2, t - w // 2 + w], 0, n)
                m[g, lo:hi, t] = 1.0 / (hi - lo)
                m[g, t, t] -= 1.0
        return m

    out["const_pool_latent"] = pool(2 * P).reshape(4, 2, P, 2 * P).transpose(2, 0, 1, 3)
    out["const_pool_prompt"] = pool(P).transpose(1, 0, 2)
    t = np.arange(2 * P)
    nf = HD // 4
    inv = 10000.0 ** (-np.arange(nf) / nf)
    cos, sin = [], []
    for at in (t // GRID_W, t % GRID_W):
        ang = at[:, None] * inv[None, :]
        cos += [np.cos(ang)] * 2
        sin += [-np.sin(ang), np.sin(ang)]
    out["const_rope"] = np.stack([np.concatenate(cos, -1), np.concatenate(sin, -1)], 1).reshape(2, P, 2, HD).transpose(1, 0, 2, 3)
    col = np.arange(2 * P) % GRID_W
    first = np.clip(col - NA_KW // 2, 0, GRID_W - NA_KW)
    seen = (col[None, :] >= first[:, None]) & (col[None, :] < first[:, None] + NA_KW)
    out["const_na_mask"] = np.where(seen, 0.0, -1e30).reshape(2, P, 2 * P).transpose(1, 0, 2)
    return {k: np.ascontiguousarray(v.astype(np.float32)) for k, v in out.items()}


def slide(table):
    import numpy as np

    off = GRID_W - NA_KW
    wide = np.pad(table, ((0, 0), (0, 0), (0, 0), (off, off)))
    return np.stack([wide[..., GRID_W - 1 - qc:2 * GRID_W - 1 - qc] for qc in range(GRID_W)], axis=2)


def kernel(**inputs):
    import numpy as _np
    import concourse.bacc as _bacc
    from concourse import mybir as _mybir
    from concourse.bass_utils import run_bass_kernel_spmd as _run

    nc = _bacc.Bacc("TRN2", target_bir_lowering=False, num_devices=1)
    arrays, args = {}, {}
    laid_out = [("na_bias_slid", slide(_np.asarray(inputs["na_bias"])))]
    for name, a in [(n, inputs[n]) for n in _INS] + laid_out + list(constants().items()):
        a = _np.ascontiguousarray(a)
        arrays[f"in_{name}_dram"] = a
        args[name] = nc.dram_tensor(f"in_{name}_dram", a.shape, _mybir.dt.from_np(a.dtype), kind="ExternalInput").ap()
    outs = [nc.dram_tensor(f"out_{i}_dram", shape, _mybir.dt.float32, kind="ExternalOutput").ap()
            for i, shape in enumerate(_OUTS)]
    program(nc, args, outs)
    r = _run(nc, [arrays], core_ids=[0])
    return tuple(r.results[0][f"out_{i}_dram"] for i in range(len(_OUTS)))
```

```python
from contextlib import ExitStack

import concourse.bass as bass
from concourse import mybir

F32 = mybir.dt.float32
U32 = mybir.dt.uint32
ALU = mybir.AluOpType
ACT = mybir.ActivationFunctionType
AX_X = mybir.AxisListType.X

P = 128
D = 1024
KC = D // P
DEPTH = 2
HD = 64
GRID_W = 64
NA_KH = 8
NA_KW = 16
NB = 3
T = NB * P
BLOCKS = list(range(NB))
KEYS = T + P
HEADS = 8
TOPK = 16
PICKS = HEADS * TOPK
N_KEYS = 128
EXPERTS = N_KEYS * N_KEYS
ALPHA = (2 * DEPTH) ** 0.25
EPS = 1e-6
WT = 256
RING = 3
SLOTS = 4
GROUP = 4
BODY = 4
LOW = -3.0e38
ADA_T, IN_T, OUT_T, Q_T = 24, 7, 4, 8
PICKS_IT = BODY * GROUP
ITS = PICKS // PICKS_IT
MAPS_BEFORE = [2, 0, 1, 1]
TAIL = 4
assert ITS == HEADS and PICKS_IT == TOPK
assert ITS * NB == ADA_T
SH1, SC1, G1, SH2, SC2, G2 = (KC * i for i in range(6))
T_AQ, T_AKV, T_FX, T_NQ, T_NK, T_NV, T_PX = range(7)
JOBS = [(b, m, h) for b in range(NB) for m in range(2) for h in range(4)]
KEY_LO = [0, P, P]
KEY_HI = [P, KEYS, KEYS]

TURNS = NB + 2 + 1 + NB + 2 * NB + 2

TOPS = Q_T + 1

INS = 5 * NB + 4


def cols_at(l):
    return ADA_T // RING + (1 + ADA_T) * l


def in_at(l, j, b):
    before = sum(2 if i in (T_NQ, T_NK) else NB for i in range(j))
    return INS * l + before + b + 1


def stream(b):
    return 0 if b == 0 else 1


class Steps:

    def __init__(self, eng):
        self.eng, self.taken, self.given = eng, {}, {}

    def take(self, sem, n=1, unit=1):
        k = self.taken[sem.name] = self.taken.get(sem.name, 0) + n
        self.eng.wait_ge(sem, k * unit)

    def free(self, sem, depth):
        k = self.taken[sem.name] = self.taken.get(sem.name, 0) + 1
        if k > depth:
            self.eng.wait_ge(sem, k - depth)

    def give(self, ins, sem):
        self.given[sem.name] = self.given.get(sem.name, 0) + 1
        ins.then_inc(sem, 1)

    def step(self, ins, sem):
        self.give(ins, sem)
        self.eng.wait_ge(sem, self.given[sem.name])


def program(nc, ins, outs):
    with ExitStack() as ctx:
        def sb(name, shape, dt=F32):
            return ctx.enter_context(nc.sbuf_tensor(name, shape, dt))

        def sem(name):
            return ctx.enter_context(nc.semaphore(name))

        ps = ctx.enter_context(nc.psum_tensor("ps", [P, 8, 512], F32))
        ps_turn = ps[:, 0:2, :].rearrange("p a n -> p (a n)")
        ps_proj = [ps[:, 2 + i, :] for i in range(2)]
        ps_sc = [ps[:, 4 + i, :] for i in range(2)]
        ps_pt = ps[:, 6, :]
        ps_o = ps[:, 7, :]
        ps_top = ps[:, 4:6, :].rearrange("p a n -> p (a n)")
        ps_y = [ps_turn, ps_top, ps_turn]
        ps_row = [ps_pt, ps_sc[0], ps_sc[1]]

        x = sb("x", [P, NB, D])
        hT = sb("hT", [P, KC, T])
        junk = sb("junk", [P, D])
        ada_tile = sb("ada_tile", [P, KC, WT])
        ada_row = [sb("ada_row", [2, WT])[:]] + [junk[0:2, 512 + i * WT:512 + (i + 1) * WT] for i in range(RING - 1)]
        h2 = sb("h2", [P, NB, D])
        xhat = h2
        mixed = junk[:, 256:256 + WT]
        mixT = sb("mixT", [P, KC, T])
        ring = sb("ring", [P, RING, KC, WT])
        ada_raw = sb("ada_raw", [P, 146])
        p_scale = ada_raw[:, 144:146]
        ada = sb("ada", [P, 6 * KC, 2])
        gate = sb("gate", [P, 2, D])
        ln_g = sb("ln_g", [P, D])
        ln_b = sb("ln_b", [P, D])
        stats = sb("stats", [P, NB, 2, 6])
        mv = sb("mv", [P, NB, 2])
        std = sb("std", [P, NB])
        rstd = sb("rstd", [P, NB])
        ident = sb("ident", [P, P])
        eps = sb("eps", [P, 1])
        zeros = sb("zeros", [P, P])
        crow = junk[0:2 * KC, 256:256 + P]
        silu_c = sb("silu_c", [P, 2, KC])
        dftL = sb("dftL", [P, 2, 2, 2 * P])
        dftP = sb("dftP", [P, 2, P])
        dftC = sb("dftC", [P, 2, P])
        poolL = sb("poolL", [P, 4, 2, 2 * P])
        poolP = sb("poolP", [P, 4, P])
        rope = sb("rope", [P, 2, 2, HD])
        na_mask = sb("na_mask", [P, 2, 2 * P])
        iota16 = sb("iota16", [P, TOPK])
        b_row = sb("b_row", [6 * KC + 2, P])
        qk_g = sb("qk_g", [P, 6, HD])
        na_b = sb("na_b", [P, 2, 4, 3 * P])
        wf = sb("wf", [P, 2, 2 * P])
        wp = sb("wp", [P, 2, HD])
        cache_k = sb("cache_k", [P, 3 * P])
        k12 = sb("k12", [P, 2, P])
        k12T = sb("k12T", [P, 2, P])
        qk = sb("qk", [P, NB, 6, HD])
        av = sb("av", [P, 4, P])
        nv = sb("nv", [P, 4, 2 * P])
        nk_out = junk[:, 0:2 * P]
        aqT = sb("aqT", [P, 2, T])
        akT = sb("akT", [P, KEYS])
        nqT = sb("nqT", [P, 2, T])
        nkT = sb("nkT", [P, 2, KEYS])
        ss = sb("ss", [P, NB, 6])
        ss2 = sb("ss2", [P, NB, 6])
        room = sb("room", [P, 2 * SLOTS * D])
        at = [0]

        def part(shape):
            n = 1
            for s in shape:
                n *= s
            v = room[:, at[0]:at[0] + n]
            at[0] += n
            assert at[0] <= 2 * SLOTS * D
            return v

        fx = part([NB, 2 * P]).rearrange("p (b n) -> p b n", b=NB)
        px = part([NB, 2 * P]).rearrange("p (b n) -> p b n", b=NB)
        dT = part([2, 2, T]).rearrange("p (c m n) -> p c m n", c=2, m=2)
        yT = part([2, T]).rearrange("p (c n) -> p c n", c=2)
        poolT = part([2, T]).rearrange("p (c n) -> p c n", c=2)
        mean_sq = at[0]
        prob = part([2, 3 * P]).rearrange("p (s n) -> p s n", s=2)
        probT = part([2, 3 * P]).rearrange("p (s n) -> p s n", s=2)
        rot = part([6, HD]).rearrange("p (h d) -> p h d", h=6)
        at[0] = mean_sq
        sq = part([NB, 6, HD]).rearrange("p (b h d) -> p b h d", b=NB, h=6)
        at[0] = 0
        u_rows = part([SLOTS, D]).rearrange("p (s n) -> p s n", s=SLOTS)
        v_rows = part([SLOTS, D]).rearrange("p (s n) -> p s n", s=SLOTS)

        nmax = sb("nmax", [P, 2])
        psums = sb("psums", [P, 2])
        pinv = sb("pinv", [P, 2])
        qT = [nqT, nkT[:, :, 0:T]]
        best = sb("best", [P, NB, 2, HEADS, TOPK])
        best_i = sb("best_i", [P, NB, 2, HEADS, TOPK], U32)
        product = hT[:].rearrange("p k n -> p (k n)")[:, 0:D]
        first_q = na_b[:].rearrange("p a h n -> p (a h n)")[:, 0:KC * WT].rearrange("p (k n) -> p k n", k=KC)
        scr = aqT[:].rearrange("p c n -> p (c n)").rearrange("p (i n) -> p i n", i=NB * 2)
        cand, cand2 = akT[:, 0:TOPK * TOPK], akT[:, TOPK * TOPK:2 * TOPK * TOPK]
        qk_flat = qk[:].rearrange("p b h d -> p (b h d)")
        at[0] = 0

        def small(shape, dt=F32):
            n = 1
            for s in shape:
                n *= s
            v = qk_flat[:, at[0]:at[0] + n]
            at[0] += n
            assert at[0] <= NB * 6 * HD
            return v if dt == F32 else v.bitcast(dt)

        same = small([2, TOPK, TOPK]).rearrange("p (a k i) -> p a k i", a=2, k=TOPK)
        pos = small([TOPK], U32)
        pos_ij = small([2, TOPK], U32).rearrange("p (a k) -> p a k", a=2)
        pos_f = small([2, TOPK]).rearrange("p (a k) -> p a k", a=2)
        best_f = small([2, TOPK]).rearrange("p (a k) -> p a k", a=2)
        found = small([2, TOPK]).rearrange("p (a k) -> p a k", a=2)
        idx_f = small([TOPK])
        top = small([TOPK])
        idx = sb("idx", [P, 2, PICKS], U32)
        cur = sb("cur", [P, BODY, GROUP], U32)
        gsum = sb("gsum", [P, HEADS])
        gw = sb("gw", [P, 2, HEADS, TOPK])
        dots = sb("dots", [P, GROUP])
        gelu = sb("gelu", [P, GROUP])
        weight = sb("weight", [P, GROUP])
        diag = sb("diag", [P, SLOTS, P])

        w_landed = [sem(f"w_landed{i}") for i in range(RING)]
        w_free = sem("w_free")
        ada_tile_in = sem("ada_tile_in")
        first_q_in = sem("first_q_in")
        row_done = sem("row_done")
        row_copied = sem("row_copied")
        col_done = sem("col_done")
        col_free = sem("col_free")
        consts_in = sem("consts_in")
        x_in = sem("x_in")
        tables_in = sem("tables_in")
        small_in = [sem(f"small_in{l}") for l in range(DEPTH)]
        small_used = sem("small_used")
        ln1_in = sem("ln1_in")
        ln2_in = sem("ln2_in")
        ln1_used = sem("ln1_used")
        ln2_used = sem("ln2_used")
        pool_ready = sem("pool_ready")
        turn_ready = sem("turn_ready")
        turn_free = sem("turn_free")
        proj_ready = sem("proj_ready")
        proj_free = sem("proj_free")
        ada_ready = sem("ada_ready")
        qk_ready = sem("qk_ready")
        gate_ready = sem("gate_ready")
        gate_used = sem("gate_used")
        dve_step = sem("dve_step")
        var_ready = sem("var_ready")
        std_ready = sem("std_ready")
        xhat_ready = sem("xhat_ready")
        hT_ready = sem("hT_ready")
        h2_ready = sem("h2_ready")
        in_ready = sem("in_ready")
        ss_ready = sem("ss_ready")
        srt_ready = sem("srt_ready")
        k_out_ready = sem("k_out_ready")
        k_out_done = sem("k_out_done")
        att_in_ready = sem("att_in_ready")
        nk_out_ready = sem("nk_out_ready")
        bias_ready = sem("bias_ready")
        side_ready = sem("side_ready")
        mix_side_ready = sem("mix_side_ready")
        s_ready = sem("s_ready")
        s_free = sem("s_free")
        nmax_ready = sem("nmax_ready")
        exp_ready = sem("exp_ready")
        prob_ready = sem("prob_ready")
        pt_ready = sem("pt_ready")
        probT_ready = sem("probT_ready")
        o_ready = sem("o_ready")
        o_free = sem("o_free")
        mo_ready = sem("mo_ready")
        mo_free = sem("mo_free")
        qT_ready = sem("qT_ready")
        top_ready = sem("top_ready")
        top_free = sem("top_free")
        gexp_in = sem("gexp_in")
        gexp_out = sem("gexp_out")
        idx_ready = [sem(f"idx_ready{i}") for i in range(2)]
        cur_ready = sem("cur_ready")
        pool_pace = sem("pool_pace")
        u_landed = [sem(f"u_landed{i}") for i in range(SLOTS)]
        v_landed = [sem(f"v_landed{i}") for i in range(SLOTS)]
        u_free = sem("u_free")
        v_free = sem("v_free")
        gelu_ready = sem("gelu_ready")
        weight_ready = sem("weight_ready")
        diag_ready = sem("diag_ready")
        y_cleared = sem("y_cleared")
        y_free = sem("y_free")
        x_ready = sem("x_ready")
        out_done = sem("out_done")

        w_view = [w.rearrange("l (k p) n -> l p k n", p=P)
                  for w in (ins["w_ada"], ins["w_in"], ins["w_out"], ins["peer_wq"])]
        table_u = ins["peer_u"].rearrange("l e d -> (l e) d")
        table_v = ins["peer_v"].rearrange("l e d -> (l e) d")

        block = ctx.enter_context(nc.Block())

        def pair_out(n):
            return (ps_o, ps_proj[1])[n // 2 % 2][:, 0:P]

        def load_small(eng, l):
            def load(dst, src, s):
                eng.dma_start(dst, src).then_inc(s, 16)

            load(b_row[0:6 * KC, :], ins["b_ada"][l].rearrange("(k p) -> k p", p=P), small_in[l])
            load(cache_k[:, 0:P], ins["cache_attn_k"][0, l].rearrange("t h d -> t (h d)"), small_in[l])
            load(cache_k[:, P:3 * P], ins["cache_na_k"][0, l].rearrange("t h d -> t (h d)"), small_in[l])
            load(av[:, 3, :], ins["cache_attn_v"][0, l].rearrange("t h d -> t (h d)"), small_in[l])
            load(nv[:, 3, :], ins["cache_na_v"][0, l].rearrange("t h d -> t (h d)"), small_in[l])
            for h in range(6):
                g = ins["q_norm_g" if h < 4 else "k_norm_g"][l:l + 1, :]
                load(qk_g[:, h, :], g.to_broadcast([P, HD]), small_in[l])
            load(wf[:], ins["w_fourier"][l].rearrange("(c p) n -> p c n", p=P), small_in[l])
            for g in range(4):
                load(wp[64 * (g % 2):64 * (g % 2) + 64, g // 2, :], ins["w_pool"][l, g], small_in[l])
            load(b_row[6 * KC:6 * KC + 2, :], ins["pool_scale"][l].rearrange("(c p) -> c p", p=P), small_in[l])
            load(k12[:, 0, :], ins["peer_k1"][l], small_in[l])
            load(k12[:, 1, :], ins["peer_k2"][l], small_in[l])
            for r in range(4):
                for h in range(4):
                    load(na_b[64 * (r % 2):64 * (r % 2) + 64, r // 2, h, 0:2 * P].rearrange("p (a b) -> p a b", a=4),
                         ins["na_bias_slid"][l, h, :, NA_KH - 1 - r:NA_KH + 3 - r, :], small_in[l])

        @block.sync
        def _(sp):
            sp.sem_inc(w_free, RING)
            with sp.Fori(0, ADA_T // RING) as i:
                for s in range(RING):
                    sp.wait_ge(w_free, i * RING + s + 1)
                    sp.dma_start(ring[:, s], w_view[0][0][:, :, bass.ds((i * RING + s) * WT, WT)]).then_inc(w_landed[s], 16)
            n = ADA_T

            def map_tile(l, i):
                if isinstance(i, int) and i == 0:
                    sp.wait_ge(mo_ready, (l + 1) * NB * OUT_T)
                sp.wait_ge(row_done, ADA_T * (l + 1) + i)
                cols_ = bass.ds(i * WT, WT) if not isinstance(i, int) else slice(i * WT, (i + 1) * WT)
                sp.dma_start(ada_tile[:], w_view[0][l + 1][:, :, cols_]).then_inc(ada_tile_in, 16)

            for l in range(DEPTH):
                maps = 0
                for w, tiles in zip(w_view[1:], (IN_T, OUT_T, Q_T)):
                    for j in range(tiles):
                        if tiles == OUT_T and j == RING:
                            if l > 0:
                                sp.wait_ge(row_done, ADA_T * (l + 1))
                            sp.dma_start(ada_tile[:], w[l][:, :, j * WT:(j + 1) * WT]).then_inc(ada_tile_in, 16)
                            continue
                        if tiles == Q_T and j == 0:
                            sp.wait_ge(s_ready, (l + 1) * len(JOBS))
                            sp.dma_start(first_q, w[l][:, :, 0:WT]).then_inc(first_q_in, 16)
                            continue
                        if tiles == Q_T and l + 1 < DEPTH and j > RING:
                            for i in range(MAPS_BEFORE[j - RING - 1]):
                                map_tile(l, maps)
                                maps += 1
                            if j == Q_T - 2:
                                sp.wait_ge(small_used, l + 1)
                                load_small(sp, l + 1)
                        sp.wait_ge(w_free, n + 1)
                        sp.dma_start(ring[:, n % RING], w[l][:, :, j * WT:(j + 1) * WT]).then_inc(w_landed[n % RING], 16)
                        n += 1
                if l + 1 < DEPTH:
                    with sp.Fori(maps, ADA_T) as i:
                        map_tile(l, i)

        @block.gpsimd
        def _(pool):
            st = Steps(pool)
            nc.gpsimd.memset(zeros[:], 0.0)
            nc.gpsimd.memset(eps[:], EPS)
            st.give(nc.gpsimd.iota(iota16[:], [[1, TOPK]], base=0, channel_multiplier=0,
                                   allow_small_or_imprecise_dtypes=True), pool_ready)
            load_small(pool, 0)
            for t, name in ((dftL, "const_dft_latent"), (dftP, "const_dft_prompt"), (dftC, "const_dft_channel"),
                            (poolL, "const_pool_latent"), (poolP, "const_pool_prompt"), (rope, "const_rope"),
                            (na_mask, "const_na_mask")):
                pool.dma_start(t[:], ins[name]).then_inc(tables_in, 16)
            pool.wait_ge(tables_in, 16 * 7)
            pool.sem_inc(u_free, SLOTS)
            pool.sem_inc(v_free, SLOTS)
            for l in range(DEPTH):
                pool.wait_ge(small_in[l], 16 * 35)
                for qb in range(2):
                    for h in range(4):
                        ins_ = nc.gpsimd.tensor_tensor(na_b[:, qb, h, 0:2 * P], na_b[:, qb, h, 0:2 * P],
                                                       na_mask[:, qb, :], ALU.add)
                ins_ = nc.gpsimd.memset(na_b[:, :, :, 2 * P:3 * P], 0.0)
                st.give(ins_, bias_ready)
                for b in range(NB):
                    step = l * NB + b

                    def copy_cur(base, g):
                        ins_ = nc.gpsimd.tensor_copy(cur[:, g % BODY, :], idx[:, step % 2, bass.ds(base * BODY * GROUP + g * GROUP, GROUP)]
                                                     if not isinstance(base, int) else
                                                     idx[:, step % 2, (base * BODY + g) * GROUP:(base * BODY + g + 1) * GROUP])
                        ins_.then_inc(cur_ready, 1)
                        pool.wait_ge(cur_ready, step * (PICKS // GROUP) + base * BODY + g + 1)
                        pool.sem_inc(pool_pace, 1)

                    def gather_u(base, g, m):
                        pool.wait_ge(u_free, step * PICKS + base * (BODY * GROUP) + g * GROUP + m + 1)
                        pool.sem_inc(pool_pace, 1)
                        nc.gpsimd.indirect_dma_start(u_rows[:, m, :], None, table_u,
                                                     bass.IndirectOffsetOnAxis(cur[:, g % BODY, m:m + 1], 0)).then_inc(u_landed[m], 16)

                    def gather_v(base, g, m):
                        pool.wait_ge(v_free, step * PICKS + base * (BODY * GROUP) + g * GROUP + m + 1)
                        pool.sem_inc(pool_pace, 1)
                        nc.gpsimd.indirect_dma_start(v_rows[:, m, :], None, table_v,
                                                     bass.IndirectOffsetOnAxis(cur[:, g % BODY, m:m + 1], 0)).then_inc(v_landed[m], 16)

                    def body(base, last):
                        for g in range(BODY):
                            ahead = not (last and g == BODY - 1)
                            if ahead:
                                if g == BODY - 1:
                                    pool.wait_ge(idx_ready[step % 2], step // 2 * HEADS + base + 2)
                                    pool.sem_inc(pool_pace, 1)
                                copy_cur(base, g + 1)
                            for m in range(GROUP):
                                if ahead:
                                    gather_u(base, g + 1, m)
                                gather_v(base, g, m)

                    pool.wait_ge(idx_ready[step % 2], step // 2 * HEADS + 1)
                    copy_cur(0, 0)
                    for m in range(GROUP):
                        gather_u(0, 0, m)
                    with pool.Fori(0, PICKS // (BODY * GROUP) - 1) as i:
                        body(i, False)
                    body(PICKS // (BODY * GROUP) - 1, True)

        @block.scalar
        def _(act):
            st = Steps(act)

            def load(dst, src, s):
                act.dma_start(dst, src).then_inc(s, 16)

            def load_ln(l, which, s):
                load(ln_g[:], ins[f"ln{which}_g"][l:l + 1, :].to_broadcast([P, D]), s)
                load(ln_b[:], ins[f"ln{which}_b"][l:l + 1, :].to_broadcast([P, D]), s)

            load(ident[:], ins["const_ident"], consts_in)
            load(crow[0:KC, :], ins["c_ctx"].rearrange("(k p) -> k p", p=P), consts_in)
            load(crow[KC:2 * KC, :], ins["c"][0].rearrange("(k p) -> k p", p=P), consts_in)
            load(x[:, 0, :], ins["x_prompt"][0], x_in)
            load(x[:, 1:3, :], ins["x_sample"][0].rearrange("(b p) d -> p b d", p=P), x_in)
            load_ln(0, 1, ln1_in)
            act.wait_ge(consts_in, 16 * 3)
            act.wait_ge(pool_ready, 1)

            act.sem_inc(col_free, 1)
            st.take(turn_ready)
            st.step(nc.scalar.activation(silu_c[:], ps_turn[:, 0:2 * KC].rearrange("p (s k) -> p s k", s=2),
                                         ACT.Silu), turn_free)

            def root(given, out, in_, scale, done):
                st.take(given)
                st.give(nc.scalar.activation(out, in_, ACT.Sqrt, bias=eps[:], scale=scale), done)

            def root_of(b):
                root(var_ready, std[:, b:b + 1], mv[:, b, 1:2], 1.0, std_ready)

            def root_all():
                root(var_ready, std[:], mv[:, :, 1], 1.0, std_ready)

            def copy_row(n, s):
                act.wait_ge(row_done, n + 1)
                nc.scalar.copy(ada_row[s], ps_row[s][0:2, 0:WT]).then_inc(row_copied, 1)

            def copy_col(n, dst, w):
                act.wait_ge(col_done, n + 1)
                nc.scalar.copy(dst, ps_o[:, 0:w]).then_inc(col_free, 1)

            def modulate(b, sh, sc):
                st.take(turn_ready)
                for k in range(KC):
                    ins_ = nc.scalar.activation(hT[:, k, b * P:(b + 1) * P], ps_turn[:, k * P:(k + 1) * P], ACT.Identity,
                                                bias=ada[:, sh + k, stream(b):stream(b) + 1],
                                                scale=ada[:, sc + k, stream(b):stream(b) + 1])
                st.step(ins_, turn_free)
                act.sem_inc(hT_ready, 1)

            def gates():
                for s in range(2):
                    st.take(turn_ready)
                    ins_ = nc.scalar.copy(gate[:, s, :], ps_turn)
                    st.step(ins_, turn_free)
                act.sem_inc(gate_ready, 1)

            for l in range(DEPTH):
                if l == 0:
                    root_all()
                    with act.Fori(0, ADA_T // RING) as i:
                        for s in range(RING):
                            copy_row(i * RING + s, s)
                        copy_col(i, ada_raw[:, bass.ds(i * 4 * RING, 4 * RING)], 4 * RING)
                copy_col(cols_at(l), ada_raw[:, 96:146], 50)
                if l > 0:
                    root_all()
                st.take(ada_ready)
                for b in range(NB):
                    modulate(b, SH1, SC1)

                def evacuate(*pairs, scale=1.0):
                    st.take(proj_ready)
                    src = ps_proj[st.taken["proj_ready"] % 2 ^ 1]
                    for dst, lo, hi in pairs:
                        part_ = src[:, lo:hi]
                        if len(dst.shape) == 4:
                            part_ = part_.rearrange("p (k g d) -> p k g d", k=2, g=2)
                        ins_ = nc.scalar.activation(dst, part_, ACT.Copy, scale=scale)
                    st.step(ins_, proj_free)
                    act.sem_inc(in_ready, 1)

                if l > 0:
                    act.wait_ge(out_done, 32 * l)
                for j in range(IN_T):
                    if j == T_PX:
                        if l > 0:
                            act.wait_ge(gate_used, l * 2)
                        gates()
                    if j in (T_NQ, T_NK):
                        for c in range(2):
                            evacuate(((nqT if j == T_NQ else nkT)[:, c, 0:T], 0, T), scale=0.125 if j == T_NQ else 1.0)
                        continue
                    for b in range(NB):
                        if j == T_AQ:
                            evacuate((qk[:, b, 0:4, :].rearrange("p (g k) d -> p k g d", g=2), 0, 256))
                        elif j == T_AKV:
                            evacuate((qk[:, b, 4:6, :].rearrange("p h d -> p (h d)"), 0, 128), (av[:, b, :], 128, 256))
                        else:
                            evacuate(({T_FX: fx, T_NV: nv, T_PX: px}[j][:, b, :], 0, 256))
                    if j == T_FX:
                        root(ss_ready, ss2[:], ss[:], 1.0 / HD, srt_ready)
                act.dma_start(outs[3][0, l].rearrange("t h d -> t (h d)"), av[:, 0, :]).then_inc(out_done, 16)
                act.dma_start(outs[5][0, l].rearrange("t h d -> t (h d)"), nv[:, 0, :]).then_inc(out_done, 16)

                st.take(turn_ready)
                nc.scalar.copy(akT[:, T:KEYS], ps_turn[:, 0:P])
                nc.scalar.copy(nkT[:, :, T:KEYS], ps_turn[:, P:3 * P].rearrange("p (c n) -> p c n", c=2))
                nc.scalar.copy(k12T[:], ps_turn[:, 512:512 + 2 * P].rearrange("p (c n) -> p c n", c=2))
                if l > 0:
                    act.wait_ge(k_out_done, 32 * l)
                st.step(nc.scalar.copy(nk_out, ps_turn[:, 768:1024]), turn_free)
                act.sem_inc(att_in_ready, 1)
                act.dma_start(outs[4][0, l].rearrange("t h d -> t (h d)"), nk_out).then_inc(k_out_done, 16)

                def side(dst, lo, hi, plo=0, phi=P, scale=1.0, final=False):
                    st.take(proj_ready)
                    src = ps_proj[st.taken["proj_ready"] % 2 ^ 1]
                    st.step(nc.scalar.activation(dst, src[plo:phi, lo:hi], ACT.Copy, scale=scale), proj_free)
                    act.sem_inc(mix_side_ready if final else side_ready, 1)

                for c in range(2):
                    for m in range(2):
                        side(dT[:, c, m, :], 0, T)
                for c in range(2):
                    side(yT[:, c, :], 0, T)
                for c in range(2):
                    side(poolT[:, c, :], 0, T)
                for c in range(2):
                    side(mixT[:, 2 + c, :], 0, T, final=True)
                for c in range(2):
                    side(mixT[:, 6 + c, :], 0, T, scale=p_scale[:, c:c + 1], final=True)

                act.wait_ge(k_out_ready, l + 1)
                act.dma_start(outs[2][0, l].rearrange("t h d -> t (h d)"),
                              qk[:, 0, 4:6, :].rearrange("p h d -> p (h d)")).then_inc(k_out_done, 16)
                for b in range(NB):
                    st.take(turn_ready)
                    nc.scalar.activation(aqT[:, :, b * P:(b + 1) * P], ps_turn[:, 0:2 * P].rearrange("p (c n) -> p c n", c=2),
                                         ACT.Copy, scale=0.125)
                    st.step(nc.scalar.copy(akT[:, b * P:(b + 1) * P], ps_turn[:, 2 * P:3 * P]), turn_free)
                    act.sem_inc(att_in_ready, 1)

                def copy_t(n):
                    b, m, h = JOBS[n]
                    w = KEY_HI[b] - KEY_LO[b]
                    st.take(pt_ready)
                    if n >= 2:
                        act.wait_ge(o_ready, l * len(JOBS) + n - 1)
                    st.step(nc.scalar.copy(probT[:, n % 2, 0:w], ps_pt[:, 0:w]), probT_ready)

                def exponent(n):
                    b, m, h = JOBS[n]
                    w = KEY_HI[b] - KEY_LO[b]
                    st.take(nmax_ready)
                    if n >= 2:
                        act.wait_ge(pt_ready, l * len(JOBS) + n - 1)
                    st.step(nc.scalar.activation(prob[:, n % 2, 0:w], ps_sc[n % 2][:, 0:w], ACT.Exp, bias=nmax[:, n % 2:n % 2 + 1],
                                                 accum_out=psums[:, n % 2:n % 2 + 1]), exp_ready)

                def head_out(n):
                    if n % 2:
                        b, m, h = JOBS[n]
                        act.wait_ge(o_ready, l * len(JOBS) + n + 1)
                        st.step(nc.scalar.copy(mixT[:, (4 if m else 0) + h // 2, b * P:(b + 1) * P], pair_out(n)), o_free)

                for n in range(len(JOBS)):
                    exponent(n)
                    if n >= 1:
                        copy_t(n - 1)
                    if n >= 2:
                        head_out(n - 2)
                copy_t(len(JOBS) - 1)
                head_out(len(JOBS) - 2)
                head_out(len(JOBS) - 1)


                def query(j, half, lo=0, hi=T):
                    st.take(proj_ready)
                    if j > 1:
                        act.wait_ge(top_ready, l * TOPS + j)
                    st.step(nc.scalar.copy(qT[j % 2][:, half, lo:hi],
                                           ps_proj[st.taken["proj_ready"] % 2 ^ 1][:, lo:hi]), proj_free)
                    act.sem_inc(qT_ready, 1)

                def back(b):
                    st.take(turn_ready)
                    st.step(nc.scalar.copy(h2[:, b, :], ps_turn), turn_free)
                    act.sem_inc(h2_ready, 1)

                def weights_exp(turn, h=slice(0, HEADS)):
                    st.take(gexp_in)
                    st.give(nc.scalar.activation(gw[:, turn % 2, h], gw[:, turn % 2, h], ACT.Exp), gexp_out)

                for b in range(NB):
                    if b < 2:
                        root_of(b)
                        root_of(b)
                    if b == 1:
                        for half in range(2):
                            query(0, half, 0, P)
                        back(0)
                        weights_exp(l * NB, 0)
                    if b < 2:
                        modulate(b, SH2, SC2)
                root_of(2)
                back(1)
                for half in range(2):
                    query(0, half, P, 2 * P)
                root_of(2)
                for half in range(2):
                    query(1, half, 0, 2 * P)
                modulate(2, SH2, SC2)
                back(2)
                for j in range(2):
                    for half in range(2):
                        query(j, half, 2 * P, T)
                act.wait_ge(gate_used, 2 * l + 1)
                gates()
                act.wait_ge(ln1_used, l + 1)
                load_ln(l, 2, ln2_in)

                def output(b):
                    if l + 1 == DEPTH:
                        act.wait_ge(x_ready, l * NB + b + 1)
                        dst = outs[0][0] if b == 0 else outs[1][0, (b - 1) * P:b * P, :]
                        act.dma_start(dst, x[:, b, :]).then_inc(out_done, 16)

                for b in range(NB):
                    step = l * NB + b

                    def iteration(i, end_last=False):
                        for g in range(BODY):
                            group(i, g)
                            if end_last and g == 1:
                                root_of(b - 1)
                            if b == 0 and 0 < i < HEADS - 1 and g == 0:
                                query(i + 1, 1)
                            if b == 0 and i + 1 < HEADS and g == 3:
                                weights_exp(step, i + 1)
                            if b == 0 and i + 2 < HEADS and g == 3:
                                query(i + 2, 0)
                            if l + 1 < DEPTH and g == 1:
                                copy_row(ADA_T + b * ITS + i, 0)
                            if l + 1 < DEPTH and g == 3:
                                dst = (bass.ds(i * 4 + b * ITS * 4, 4) if not isinstance(i, int) else
                                       slice((b * ITS + i) * 4, (b * ITS + i + 1) * 4))
                                copy_col(ADA_T // RING + 1 + b * ITS + i, ada_raw[:, dst], 4)

                    def group(base, g):
                        first = step * PICKS + base * (BODY * GROUP) + g * GROUP
                        turn = step * (PICKS // GROUP) + base * BODY + g
                        act.wait_ge(u_free, first + GROUP + SLOTS)
                        nc.scalar.activation(gelu[:], dots[:], ACT.Gelu).then_inc(gelu_ready, 1)
                        act.wait_ge(weight_ready, turn + 1)
                        for m in range(GROUP):
                            act.wait_ge(v_free, first + m + 1)
                            nc.scalar.activation(diag[:, m, :], ident[:], ACT.Copy,
                                                 scale=weight[:, m:m + 1]).then_inc(diag_ready, 1)

                    iteration(0, end_last=b > 0)
                    if b > 0:
                        output(b - 1)
                    if b == 0:
                        for i in range(1, ITS):
                            iteration(i)
                    else:
                        with act.Fori(1, ITS) as i:
                            iteration(i)
                    if b + 1 < NB:
                        weights_exp(step + 1)
                root_of(NB - 1)
                output(NB - 1)
                if l + 1 < DEPTH:
                    act.wait_ge(ln2_used, l + 1)
                    load_ln(l + 1, 1, ln1_in)
            act.wait_ge(out_done, 16 * (2 * DEPTH + NB))
            act.wait_ge(k_out_done, 32 * DEPTH)

        @block.vector
        def _(dve):
            st = Steps(dve)
            V = nc.vector

            def step(ins_):
                st.step(ins_, dve_step)

            dve.wait_ge(consts_in, 16 * 3)
            dve.wait_ge(pool_ready, 1)

            def spread(bs):
                for b in bs:
                    for half in range(2):
                        ins_ = V.bn_stats(stats[:, b, half, :], x[:, b, half * 512:(half + 1) * 512])
                step(ins_)
                for b in bs:
                    ins_ = V.bn_aggr(mv[:, b, :], stats[:, b].rearrange("p a b -> p (a b)"))
                st.step(ins_, var_ready)

            def inverse(bs):
                st.take(std_ready)
                step(V.reciprocal(rstd[:, bs[0]:bs[-1] + 1], std[:, bs[0]:bs[-1] + 1]))

            def normalize(dst, b):
                return V.tensor_scalar(dst, x[:, b, :], mv[:, b, 0:1], rstd[:, b:b + 1], ALU.subtract, ALU.mult)

            def post_norm(b, final):
                inverse([b])
                step(normalize(x[:, b, :], b))
                step(V.tensor_tensor(x[:, b, :], x[:, b, :], ln_g[:], ALU.mult))
                st.step(V.tensor_tensor(x[:, b, :], x[:, b, :], ln_b[:], ALU.add), final)

            def normalized(bs=BLOCKS):
                spread(bs)
                inverse(bs)
                for b in bs:
                    st.step(normalize(xhat[:, b, :], b), xhat_ready)

            for l in range(DEPTH):
                if l == 0:
                    dve.wait_ge(x_in, 16 * 2)
                    normalized()
                    dve.wait_ge(tables_in, 16 * 7)
                dve.wait_ge(small_in[l], 16 * 35)
                dve.wait_ge(col_free, cols_at(l) + 2)
                step(V.tensor_tensor(ada[:], ada_raw[:, 0:96].rearrange("p (c s) -> p c s", s=2),
                                     ada_raw[:, 96:144].unsqueeze(2).to_broadcast([P, 6 * KC, 2]), ALU.add))
                V.tensor_scalar(ada[:, SC1:SC1 + KC, :], ada[:, SC1:SC1 + KC, :], 1.0, None, ALU.add)
                st.step(V.tensor_scalar(ada[:, SC2:SC2 + KC, :], ada[:, SC2:SC2 + KC, :], 1.0, None, ALU.add), ada_ready)

                if l > 0:
                    normalized()

                dve.wait_ge(in_ready, in_at(l, T_AKV, NB - 1))
                step(V.tensor_tensor(sq, qk[:], qk[:], ALU.mult))
                st.step(V.tensor_reduce(ss[:], sq, AX_X, ALU.add), ss_ready)
                st.take(srt_ready)
                step(V.reciprocal(ss[:], ss2[:]))
                step(V.tensor_tensor(qk[:], qk[:], ss[:].unsqueeze(3).to_broadcast([P, NB, 6, HD]), ALU.mult))
                st.step(V.tensor_tensor(qk[:], qk[:], qk_g[:].unsqueeze(1).to_broadcast([P, NB, 6, HD]), ALU.mult), k_out_ready)
                for b in range(1, NB):
                    cos = rope[:, b - 1, 0, :].unsqueeze(1).to_broadcast([P, 6, HD])
                    sin = rope[:, b - 1, 1, :].rearrange("p (e d) -> p e d", e=4)
                    r5 = rot.rearrange("p h (e d) -> p h e d", e=4)
                    s5 = qk[:, b].rearrange("p h (e d) -> p h e d", e=4)
                    for e in range(4):
                        ins_ = V.tensor_tensor(r5[:, :, e, :], s5[:, :, e ^ 1, :],
                                               sin[:, e, :].unsqueeze(1).to_broadcast([P, 6, 16]), ALU.mult)
                    step(ins_)
                    step(V.tensor_tensor(qk[:, b], qk[:, b], cos, ALU.mult))
                    st.step(V.tensor_tensor(qk[:, b], qk[:, b], rot, ALU.add), qk_ready)

                J = len(JOBS)

                def maximum(n):
                    b, m, h = JOBS[n]
                    w = KEY_HI[b] - KEY_LO[b]
                    st.take(s_ready)
                    src = ps_sc[n % 2][:, 0:w]
                    st.step(V.tensor_reduce(nmax[:, n % 2:n % 2 + 1], src, AX_X, ALU.max, negate=True), nmax_ready)

                def divide(n):
                    b, m, h = JOBS[n]
                    w = KEY_HI[b] - KEY_LO[b]
                    st.take(exp_ready)
                    step(V.reciprocal(pinv[:, n % 2:n % 2 + 1], psums[:, n % 2:n % 2 + 1]))
                    st.step(V.tensor_scalar(prob[:, n % 2, 0:w], prob[:, n % 2, 0:w], pinv[:, n % 2:n % 2 + 1], None,
                                            ALU.mult), prob_ready)

                maximum(0)
                for n in range(J):
                    divide(n)
                    if n + 1 < J:
                        maximum(n + 1)

                st.take(gate_ready)
                def pick(b, h):
                    turn = l * NB + b
                    step(V.tensor_tensor(cand.rearrange("p (i j) -> p i j", i=TOPK),
                                         best[:, b, 0, h].unsqueeze(2).to_broadcast([P, TOPK, TOPK]),
                                         best[:, b, 1, h].unsqueeze(1).to_broadcast([P, TOPK, TOPK]), ALU.add))
                    step(V.max(top[:, 0:8], cand))
                    V.max_index(pos[:, 0:8], top[:, 0:8], cand)
                    step(V.match_replace(cand2, top[:, 0:8], cand, LOW))
                    step(V.max(top[:, 8:16], cand2))
                    step(V.max_index(pos[:, 8:16], top[:, 8:16], cand2))
                    ins_ = V.tensor_tensor(gw[:, turn % 2, h], top, top[:, 0:1].to_broadcast([P, TOPK]), ALU.subtract)
                    if b == 0 or h == HEADS - 1:
                        st.give(ins_, gexp_in)
                    V.tensor_scalar(pos_ij[:, 0], pos, 4, None, ALU.logical_shift_right)
                    V.tensor_scalar(pos_ij[:, 1], pos, 15, None, ALU.bitwise_and)
                    step(V.tensor_copy(best_f, best_i[:, b, :, h]))
                    step(V.tensor_copy(pos_f, pos_ij))
                    full = [P, 2, TOPK, TOPK]
                    step(V.tensor_tensor(same, pos_f.unsqueeze(3).to_broadcast(full),
                                         iota16[:].unsqueeze(1).unsqueeze(1).to_broadcast(full), ALU.is_equal))
                    step(V.tensor_tensor(same, same, best_f.unsqueeze(2).to_broadcast(full), ALU.mult))
                    step(V.tensor_reduce(found, same, AX_X, ALU.add))
                    step(V.tensor_scalar(idx_f, found[:, 0], float(N_KEYS), float(l * EXPERTS), ALU.mult, ALU.add))
                    st.step(V.tensor_tensor(idx[:, turn % 2, h * TOPK:(h + 1) * TOPK], idx_f, found[:, 1], ALU.add), idx_ready[turn % 2])

                def sides(j, bs):
                    return [(2 * b + half, b, half, (ps_pt if j == 0 and b == 0 else ps_top)[:, (2 * b + half) * P:(2 * b + half + 1) * P])
                            for b in bs for half in range(2)]

                def best_eight(j, bs=BLOCKS):
                    st.take(top_ready)
                    for i, b, half, scores in sides(j, bs):
                        ins_ = V.max(best[:, b, half, j, 0:8], scores)
                    step(ins_)
                    for i, b, half, scores in sides(j, bs):
                        V.max_index(best_i[:, b, half, j, 0:8], best[:, b, half, j, 0:8], scores)
                        ins_ = V.match_replace(scr[:, i, :], best[:, b, half, j, 0:8], scores, LOW)
                    st.step(ins_, top_free)

                def next_eight(j, bs=BLOCKS):
                    for i, b, half, scores in sides(j, bs):
                        ins_ = V.max(best[:, b, half, j, 8:16], scr[:, i, :])
                    step(ins_)
                    for i, b, half, scores in sides(j, bs):
                        ins_ = V.max_index(best_i[:, b, half, j, 8:16], best[:, b, half, j, 8:16], scr[:, i, :])
                    step(ins_)

                def shares(turn, h):
                    st.take(gexp_out)
                    n = h.stop - h.start
                    step(V.tensor_reduce(gsum[:, h], gw[:, turn % 2, h], AX_X, ALU.add))
                    step(V.reciprocal(gsum[:, h], gsum[:, h]))
                    step(V.tensor_tensor(gw[:, turn % 2, h], gw[:, turn % 2, h],
                                         gsum[:, h].unsqueeze(2).to_broadcast([P, n, TOPK]), ALU.mult))

                st.take(ln1_in, 2, 16)
                dve.wait_ge(k_out_done, 32 * (l + 1))
                for b in range(NB):
                    for j in range(OUT_T):
                        c = slice(j * WT, (j + 1) * WT)
                        st.take(mo_ready)
                        st.step(V.tensor_tensor(mixed, ps_sc[(b * OUT_T + j) % 2][:, 0:WT], gate[:, stream(b), c], ALU.mult), mo_free)
                        step(V.scalar_tensor_tensor(x[:, b, c], x[:, b, c], ALPHA, mixed, ALU.mult, ALU.add))
                    spread([b])
                    post_norm(b, dve_step)
                    if b == NB - 1:
                        dve.sem_inc(gate_used, 1)
                        dve.sem_inc(ln1_used, 1)
                    normalized([b])
                    if b == 1:
                        best_eight(0, [0])
                        next_eight(0, [0])
                        pick(0, 0)
                for b in range(NB):
                    turn = l * NB + b
                    st.take(h2_ready)
                    if b > 0:
                        shares(turn, slice(0, HEADS))
                    gflat = gw[:, turn % 2].rearrange("p h k -> p (h k)")

                    def group(base, g):
                        first = turn * PICKS + base * (BODY * GROUP) + g * GROUP
                        for m in range(GROUP):
                            row = turn * (PICKS // SLOTS) + base * BODY + g
                            dve.wait_ge(u_landed[m], (row + 1) * 16)
                            dve.wait_ge(u_free, first + m + SLOTS)
                            V.tensor_tensor_reduce(out=junk[:], in0=u_rows[:, m, :], in1=h2[:, b, :], scale=1.0, scalar=0.0,
                                                   op0=ALU.mult, op1=ALU.add, accum_out=dots[:, m:m + 1]).then_inc(u_free, 1)
                        if b == 0 and g == 0:
                            shares(turn, slice(base, base + 1))
                        dve.wait_ge(gelu_ready, turn * (PICKS // GROUP) + base * BODY + g + 1)
                        at_ = (bass.ds(base * (BODY * GROUP) + g * GROUP, GROUP) if not isinstance(base, int) else
                               slice((base * BODY + g) * GROUP, (base * BODY + g + 1) * GROUP))
                        V.tensor_tensor(weight[:], gelu[:], gflat[:, at_], ALU.mult).then_inc(weight_ready, 1)
                        dve.wait_ge(weight_ready, turn * (PICKS // GROUP) + base * BODY + g + 1)

                    def update(b):
                        last = l * NB + b
                        dve.wait_ge(v_free, (last + 1) * PICKS + SLOTS)
                        st.step(V.tensor_tensor(product, ps_y[b], gate[:, stream(b), :], ALU.mult), y_free)
                        step(V.scalar_tensor_tensor(x[:, b, :], x[:, b, :], ALPHA, product, ALU.mult, ALU.add))
                        spread([b])

                    def iteration(i, ahead, end_last=False):
                        for g in range(BODY):
                            group(i, g)
                            if b == 0 and i == 0 and g == 0:
                                best_eight(0, [1, 2])
                                next_eight(0, [1, 2])
                                st.take(gate_ready)
                                st.take(ln2_in, 2, 16)
                            if b == 0 and i + 1 < HEADS and g == 1:
                                best_eight(i + 1)
                                next_eight(i + 1)
                            if b == 0 and i + 1 < HEADS and g == 2:
                                pick(0, i + 1)
                            if ahead and g in (0, 3):
                                pick(b + 1, (i - ITS + TAIL) * 2 + g // 3)
                            if end_last and g == 0:
                                update(b - 1)
                            if end_last and g == 2:
                                post_norm(b - 1, x_ready)

                    more = b + 1 < NB
                    if b == 0:
                        for i in range(ITS):
                            iteration(i, i >= ITS - TAIL)
                    else:
                        iteration(0, False, end_last=True)
                        with dve.Fori(1, ITS - TAIL if more else ITS) as i:
                            iteration(i, False)
                        for i in range(ITS - TAIL, ITS) if more else ():
                            iteration(i, True)
                update(NB - 1)
                post_norm(NB - 1, x_ready)
                dve.sem_inc(gate_used, 1)
                dve.sem_inc(ln2_used, 1)

        @block.tensor
        def _(pe):
            st = Steps(pe)
            M = nc.tensor

            zero_by = dftL[:].rearrange("p m k n -> p (m k n)")
            tiles = [ADA_T]

            def weights():
                n = tiles[0]
                tiles[0] += 1
                pe.wait_ge(w_landed[n % RING], 16 * (n // RING + 1))
                return ring[:, n % RING]

            def rows(w, s):
                for k in range(KC):
                    ins_ = M.matmul(ps_row[s][0:2, 0:WT], silu_c[:, :, k], w[:, k, :], start=(k == 0), stop=(k == KC - 1))
                return ins_

            def cols(s):
                for m in range(2):
                    ins_ = M.matmul(ps_o[:, 4 * s + 2 * m:4 * s + 2 * m + 2], ada_row[s][:, m * P:(m + 1) * P], ident[0:2, 0:2],
                                    start=True, stop=True)
                return ins_

            projs = [0]

            def proj():
                st.free(proj_free, 2)
                projs[0] += 1
                return ps_proj[(projs[0] - 1) % 2]

            def turn_in():
                st.free(turn_free, 1)

            pe.wait_ge(consts_in, 16 * 3)
            pe.wait_ge(pool_ready, 1)
            turn_in()
            st.give(M.transpose(ps_turn[:, 0:2 * KC], crow, ident[0:2 * KC, 0:2 * KC]), turn_ready)
            pe.wait_ge(turn_free, 1)

            def transposes(b):
                for k in range(KC):
                    ins_ = M.transpose(ps_turn[:, k * P:(k + 1) * P], xhat[:, b, k * P:(k + 1) * P], ident[:])
                st.give(ins_, turn_ready)

            def gates(g):
                for s in range(2):
                    turn_in()
                    for k in range(KC):
                        ins_ = M.matmul(ps_turn[:, k * P:(k + 1) * P], ada[:, g + k, s:s + 1].to_broadcast([P, P]), ident[:],
                                        start=True, stop=True)
                    st.give(ins_, turn_ready)

            for l in range(DEPTH):
                J = len(JOBS)
                if l == 0:
                    with pe.Fori(0, ADA_T // RING) as i:
                        for s in range(RING):
                            pe.wait_ge(w_landed[s], (i + 1) * 16)
                            rows(ring[:, s], s).then_inc(row_done, 1)
                        pe.wait_ge(col_free, i + 1)
                        for s in range(RING):
                            pe.wait_ge(row_copied, i * RING + s + 1)
                            pe.sem_inc(w_free, 1)
                            ins_ = cols(s)
                        ins_.then_inc(col_done, 1)
                if l == 0:
                    pe.wait_ge(tables_in, 16 * 7)
                pe.wait_ge(small_in[l], 16 * 35)
                pe.wait_ge(col_free, cols_at(l) + 1)
                M.transpose(ps_o[:, 0:50], b_row[:], ident[0:6 * KC + 2, 0:6 * KC + 2]).then_inc(col_done, 1)
                if l > 0:
                    pe.wait_ge(y_free, NB * l)

                def project(b, w):
                    out = proj()
                    for k in range(KC):
                        ins_ = M.matmul(out[:, 0:WT], hT[:, k, b * P:(b + 1) * P], w[:, k, :], start=(k == 0), stop=(k == KC - 1))
                    st.give(ins_, proj_ready)

                def used():
                    pe.wait_ge(proj_ready, st.given["proj_ready"])
                    pe.sem_inc(w_free, 1)

                for b in range(NB + 1):
                    if b < NB:
                        st.take(xhat_ready)
                        turn_in()
                        transposes(b)
                    if b == 0:
                        w = weights()
                    else:
                        st.take(hT_ready)
                        project(b - 1, w)
                used()
                for j in range(1, IN_T):
                    if j == T_PX:
                        st.take(ada_ready)
                        gates(G1)
                    w = weights()
                    if j in (T_NQ, T_NK):
                        for c in range(2):
                            out = proj()
                            for k in range(KC):
                                ins_ = M.matmul(out[:, 0:T], w[:, k, c * P:(c + 1) * P], hT[:, k, :], start=(k == 0), stop=(k == KC - 1))
                            st.give(ins_, proj_ready)
                    else:
                        for b in range(NB):
                            project(b, w)
                    used()

                pe.wait_ge(in_ready, in_at(l, T_PX, NB - 1))
                turn_in()
                for c in range(3):
                    M.transpose(ps_turn[:, c * P:(c + 1) * P], cache_k[:, c * P:(c + 1) * P], ident[:])
                for c in range(2):
                    M.transpose(ps_turn[:, 512 + c * P:512 + (c + 1) * P], k12[:, c, :], ident[:])
                for c in range(2):
                    ins_ = M.transpose(ps_turn[:, 768 + c * P:768 + (c + 1) * P], nkT[:, c, 0:P], ident[:])
                st.give(ins_, turn_ready)

                for c in range(2):
                    for m in range(2):
                        out = proj()
                        cc = slice(c * P, (c + 1) * P)
                        M.matmul(out[:, 0:P], fx[:, 0, cc], dftP[:, m, :], start=True, stop=True)
                        for k in range(2):
                            ins_ = M.matmul(out[:, P:T], fx[:, 1 + k, cc], dftL[:, m, k, :], start=(k == 0), stop=(k == 1))
                        st.give(ins_, proj_ready)
                st.take(side_ready, 4)
                for c in range(2):
                    out = proj()
                    for m in range(2):
                        ins_ = M.matmul(out[:, 0:T], dftC[:, m, :], dT[:, c, m, :], start=(m == 0), stop=(m == 1))
                    st.give(ins_, proj_ready)
                for c in range(2):
                    out = proj()
                    for g in (2 * c, 2 * c + 1):
                        lo, cc = 64 * (g % 2), slice(g * HD, (g + 1) * HD)
                        M.matmul(out[lo:lo + 64, 0:P], px[:, 0, cc], poolP[:, g, :], start=True, stop=True)
                        for k in range(2):
                            ins_ = M.matmul(out[lo:lo + 64, P:T], px[:, 1 + k, cc], poolL[:, g, k, :], start=(k == 0), stop=(k == 1))
                    st.give(ins_, proj_ready)
                st.take(side_ready, 2)
                for c in range(2):
                    out = proj()
                    for k in range(2):
                        ins_ = M.matmul(out[:, 0:T], wf[:, k, c * P:(c + 1) * P], yT[:, k, :], start=(k == 0), stop=(k == 1))
                    st.give(ins_, proj_ready)
                st.take(side_ready, 2)
                for c in range(2):
                    out = proj()
                    for lo in (0, 64):
                        ins_ = M.matmul(out[lo:lo + 64, 0:T], wp[lo:lo + 64, c, :], poolT[lo:lo + 64, c, :], start=True, stop=True)
                    st.give(ins_, proj_ready)

                for b in range(NB):
                    if b == 0:
                        pe.wait_ge(k_out_ready, l + 1)
                    else:
                        st.take(qk_ready)
                    turn_in()
                    for g in range(2):
                        M.transpose(ps_turn[:, g * P:(g + 1) * P], qk[:, b, 2 * g:2 * g + 2, :].rearrange("p h d -> p (h d)"), ident[:])
                    st.give(M.transpose(ps_turn[:, 2 * P:3 * P], qk[:, b, 4:6, :].rearrange("p h d -> p (h d)"), ident[:]), turn_ready)

                pe.wait_ge(att_in_ready, (l + 1) * (1 + NB))
                st.take(bias_ready)

                def scores(n):
                    b, m, h = JOBS[n]
                    lo, hi = KEY_LO[b], KEY_HI[b]
                    q, keys = (nqT, nkT[:, h // 2, :]) if m else (aqT, akT)
                    r, c = (h % 2, h // 2) if m else (h // 2, h % 2)
                    if n >= 2:
                        pe.wait_ge(exp_ready, l * J + n - 1)
                    near = m and b
                    ins_ = M.matmul(ps_sc[n % 2][:, 0:hi - lo], q[64 * r:64 * r + 64, c, b * P:(b + 1) * P],
                                    keys[64 * r:64 * r + 64, lo:hi], start=True, stop=not near)
                    if near:
                        ins_ = M.matmul(ps_sc[n % 2][:, 0:hi - lo], ident[:], na_b[:, b - 1, h, :], start=False, stop=True)
                    st.give(ins_, s_ready)

                def turn_probs(n):
                    b, m, h = JOBS[n]
                    st.take(prob_ready)
                    if n >= 1:
                        pe.wait_ge(probT_ready, l * J + n)
                    for k in range((KEY_HI[b] - KEY_LO[b]) // P):
                        ins_ = M.transpose(ps_pt[:, k * P:(k + 1) * P], prob[:, n % 2, k * P:(k + 1) * P], ident[:])
                    st.give(ins_, pt_ready)

                def values(n):
                    b, m, h = JOBS[n]
                    st.take(probT_ready)
                    if n % 2 == 0:
                        st.free(o_free, 2)
                    if n == 2:
                        st.take(mix_side_ready, 4)
                    nk = (KEY_HI[b] - KEY_LO[b]) // P
                    lo = 64 * (h % 2)
                    v = nv[:, :, h * HD:(h + 1) * HD] if m else av[:, :, (h // 2) * HD:(h // 2 + 1) * HD]
                    for k in range(nk):
                        ins_ = M.matmul(pair_out(n)[lo:lo + 64, :], v[:, KEY_LO[b] // P + k, :], probT[:, n % 2, k * P:(k + 1) * P],
                                        start=(k == 0), stop=(k == nk - 1))
                    st.give(ins_, o_ready)

                scores(0)
                for n in range(J):
                    if n + 1 < J:
                        scores(n + 1)
                    turn_probs(n)
                    if n >= 1:
                        values(n - 1)
                values(J - 1)

                pe.wait_ge(o_free, (l + 1) * J // 2)
                ws = [weights() for j in range(RING)] + [ada_tile]
                pe.wait_ge(ada_tile_in, 16 * (l * (1 + ADA_T) + 1))

                def norm_turn(b):
                    st.take(xhat_ready)
                    turn_in()
                    transposes(b)

                def out(b, j):
                    st.free(mo_free, 2)
                    for k in range(KC):
                        ins_ = M.matmul(ps_sc[(b * OUT_T + j) % 2][:, 0:WT], mixT[:, k, b * P:(b + 1) * P], ws[j][:, k, :],
                                        start=(k == 0), stop=(k == KC - 1))
                    st.give(ins_, mo_ready)

                def key_scores(j, bs=BLOCKS):
                    st.take(qT_ready, 4 if bs == [1, 2] or j == 1 else 2)
                    st.free(top_free, 1)
                    for b in bs:
                        to = ps_pt if bs == [0] else ps_top
                        for half in range(2):
                            i = b * 2 + half
                            ins_ = M.matmul(to[:, i * P:(i + 1) * P], qT[j % 2][:, half, b * P:(b + 1) * P], k12T[:, half, :],
                                            start=True, stop=True)
                    st.give(ins_, top_ready)

                def query(half, w, lo=0, hi=T):
                    to = proj()
                    for k in range(KC):
                        ins_ = M.matmul(to[:, lo:hi], w[:, k, half * P:(half + 1) * P], hT[:, k, lo:hi], start=(k == 0), stop=(k == KC - 1))
                    st.give(ins_, proj_ready)

                def back(b):
                    turn_in()
                    for k in range(KC):
                        ins_ = M.transpose(ps_turn[:, k * P:(k + 1) * P], hT[:, k, b * P:(b + 1) * P], ident[:])
                    st.give(ins_, turn_ready)

                for b in range(2):
                    for j in range(OUT_T):
                        out(b, j)
                norm_turn(0)
                out(2, 0)
                pe.wait_ge(first_q_in, 16 * (l + 1))
                st.take(hT_ready)
                for half in range(2):
                    query(half, first_q, 0, P)
                back(0)
                key_scores(0, [0])
                for j in range(1, OUT_T):
                    out(2, j)
                pe.wait_ge(mo_ready, st.given["mo_ready"])
                pe.sem_inc(w_free, RING)
                norm_turn(1)
                st.take(hT_ready)
                back(1)
                for half in range(2):
                    query(half, first_q, P, 2 * P)
                w = weights()
                for half in range(2):
                    query(half, w, 0, 2 * P)
                norm_turn(2)
                st.take(hT_ready)
                back(2)
                for tile in (first_q, w):
                    for half in range(2):
                        query(half, tile, 2 * P, T)
                used()
                gates(G2)
                pe.wait_ge(mo_free, (l + 1) * OUT_T * NB)
                key_scores(0, [1, 2])
                pe.wait_ge(top_ready, l * TOPS + 2)
                pe.sem_inc(small_used, 1)
                for b in range(NB):
                    turn = l * NB + b
                    y = ps_y[b]
                    if b == 0:
                        pe.wait_ge(turn_free, 1 + TURNS * (l + 1))
                    if b == 1:
                        pe.wait_ge(top_free, TOPS * (l + 1))
                    if turn >= 2:
                        pe.wait_ge(y_free, turn - 1)
                    for half in range(2):
                        M.matmul(y[:, half * 512:(half + 1) * 512], zeros[:], zero_by[:, half * 512:(half + 1) * 512],
                                 start=True, stop=True, skip_group_check=True)

                    def group(base, g):
                        first = turn * PICKS + base * (BODY * GROUP) + g * GROUP
                        for m in range(GROUP):
                            pe.wait_ge(diag_ready, first + m + 1)
                            pe.wait_ge(v_landed[m], (turn * (PICKS // SLOTS) + base * BODY + g + 1) * 16)
                            for half in range(2):
                                ins_ = M.matmul(y[:, half * 512:(half + 1) * 512], diag[:, m, :],
                                                v_rows[:, m, half * 512:(half + 1) * 512], start=False, stop=True,
                                                skip_group_check=True)
                            ins_.then_inc(v_free, 1)

                    def next_map(i, g):
                        n = b * ITS + i
                        if g == 0:
                            pe.wait_ge(ada_tile_in, 16 * (l * (1 + ADA_T) + 1 + n + 1))
                            rows(ada_tile, 0).then_inc(row_done, 1)
                        if g == 2:
                            pe.wait_ge(row_copied, n + ADA_T + 1)
                            pe.wait_ge(col_free, n + ADA_T // RING + 2)
                            cols(0).then_inc(col_done, 1)

                    def iteration(i):
                        for g in range(BODY):
                            group(i, g)
                            if b == 0 and i < HEADS - 1 and g == 0:
                                key_scores(i + 1)
                            if b == 0 and i + 2 < HEADS and g > 1:
                                if g == 2:
                                    w = weights()
                                query(g - 2, w)
                                if g == 3:
                                    used()
                            if l + 1 < DEPTH:
                                next_map(i, g)

                    if b == 0:
                        for i in range(ITS):
                            iteration(i)
                    else:
                        with pe.Fori(0, ITS) as i:
                            iteration(i)


_INS = ["x_prompt", "x_sample", "cache_attn_k", "cache_attn_v", "cache_na_k", "cache_na_v", "c", "c_ctx", "w_ada", "b_ada",
        "w_in", "q_norm_g", "k_norm_g", "w_fourier", "w_pool", "pool_scale", "w_out", "ln1_g", "ln1_b",
        "ln2_g", "ln2_b", "peer_wq", "peer_k1", "peer_k2", "peer_u", "peer_v"]
_OUTS = [(1, 128, 1024), (1, 256, 1024), (1, 2, 128, 2, 64), (1, 2, 128, 2, 64), (1, 2, 128, 4, 64), (1, 2, 128, 4, 64)]


def constants():
    import numpy as np

    def dft(n):
        a = 2 * np.pi * (np.outer(np.arange(n), np.arange(n)) % n) / n
        return np.cos(a), np.sin(a)

    out = {"const_ident": np.eye(P)}
    c, s = (t / np.sqrt(2 * P * HD) for t in dft(2 * P))
    out["const_dft_latent"] = np.stack([c, s]).reshape(2, 2, P, 2 * P).transpose(2, 0, 1, 3)
    c, s = (t / np.sqrt(P * HD) for t in dft(P))
    out["const_dft_prompt"] = np.stack([c, s]).transpose(1, 0, 2)
    c, s = dft(HD)
    out["const_dft_channel"] = np.stack([np.kron(np.eye(2), c), np.kron(np.eye(2), -s)]).transpose(1, 0, 2)

    def pool(n):
        m = np.zeros((4, n, n))
        for g, w in enumerate((2, 4, 8, 16)):
            for t in range(n):
                lo, hi = np.clip([t - w // 2, t - w // 2 + w], 0, n)
                m[g, lo:hi, t] = 1.0 / (hi - lo)
                m[g, t, t] -= 1.0
        return m

    out["const_pool_latent"] = pool(2 * P).reshape(4, 2, P, 2 * P).transpose(2, 0, 1, 3)
    out["const_pool_prompt"] = pool(P).transpose(1, 0, 2)
    t = np.arange(2 * P)
    nf = HD // 4
    inv = 10000.0 ** (-np.arange(nf) / nf)
    cos, sin = [], []
    for at in (t // GRID_W, t % GRID_W):
        ang = at[:, None] * inv[None, :]
        cos += [np.cos(ang)] * 2
        sin += [-np.sin(ang), np.sin(ang)]
    out["const_rope"] = np.stack([np.concatenate(cos, -1), np.concatenate(sin, -1)], 1).reshape(2, P, 2, HD).transpose(1, 0, 2, 3)
    col = np.arange(2 * P) % GRID_W
    first = np.clip(col - NA_KW // 2, 0, GRID_W - NA_KW)
    seen = (col[None, :] >= first[:, None]) & (col[None, :] < first[:, None] + NA_KW)
    out["const_na_mask"] = np.where(seen, 0.0, -1e30).reshape(2, P, 2 * P).transpose(1, 0, 2)
    return {k: np.ascontiguousarray(v.astype(np.float32)) for k, v in out.items()}


def slide(table):
    import numpy as np

    off = GRID_W - NA_KW
    wide = np.pad(table, ((0, 0), (0, 0), (0, 0), (off, off)))
    return np.stack([wide[..., GRID_W - 1 - qc:2 * GRID_W - 1 - qc] for qc in range(GRID_W)], axis=2)


def kernel(**inputs):
    import numpy as _np
    import concourse.bacc as _bacc
    from concourse import mybir as _mybir
    from concourse.bass_utils import run_bass_kernel_spmd as _run

    nc = _bacc.Bacc("TRN2", target_bir_lowering=False, num_devices=1)
    arrays, args = {}, {}
    laid_out = [("na_bias_slid", slide(_np.asarray(inputs["na_bias"])))]
    for name, a in [(n, inputs[n]) for n in _INS] + laid_out + list(constants().items()):
        a = _np.ascontiguousarray(a)
        arrays[f"in_{name}_dram"] = a
        args[name] = nc.dram_tensor(f"in_{name}_dram", a.shape, _mybir.dt.from_np(a.dtype), kind="ExternalInput").ap()
    outs = [nc.dram_tensor(f"out_{i}_dram", shape, _mybir.dt.float32, kind="ExternalOutput").ap()
            for i, shape in enumerate(_OUTS)]
    program(nc, args, outs)
    r = _run(nc, [arrays], core_ids=[0])
    return tuple(r.results[0][f"out_{i}_dram"] for i in range(len(_OUTS)))
```
